# Optimizing a Trainium2 kernel written in Bass

```python
import math
import jax, jax.numpy as jnp
from jax import lax
import numpy as np

D_MODEL = 1024
BATCH = 1
SEQ = 256
DEPTH = 2

N_MIXERS = 2
MIX_WIDTH = 2 * D_MODEL
EPS = 1e-6

MEM_LEN = 256
MEM_HEADS = 4
MEM_WIDTH = MIX_WIDTH // 4
MEM_HEAD_DIM = MEM_WIDTH // MEM_HEADS

SSD_HEAD_DIM = 64
SSD_INNER = MIX_WIDTH - MEM_WIDTH
SSD_HEADS = SSD_INNER // SSD_HEAD_DIM
SSD_GROUPS = 4
SSD_HEADS_PER_GROUP = SSD_HEADS // SSD_GROUPS
SSD_STATE = 128
SSD_CONV = 4
SSD_CHUNK = 128
SSD_CONV_DIM = SSD_INNER + 2 * SSD_GROUPS * SSD_STATE
SSD_IN = SSD_INNER + SSD_CONV_DIM + SSD_HEADS + MEM_WIDTH

SB_HEAD_DIM = 128
SB_WIDTH = MIX_WIDTH - MEM_WIDTH
SB_HEADS = SB_WIDTH // SB_HEAD_DIM
SB_BLOCK = 128
SB_IN = 3 * SB_WIDTH + MEM_WIDTH

FFN_HIDDEN = ((-(-8 * D_MODEL // 3) + 255) // 256) * 256

N_SSD_LAYERS = (DEPTH + 1) // 2
N_SB_LAYERS = DEPTH // 2

kernel_name = "hybrid_ssd_stickbreak_memxattn_trunk"

def _rmsnorm(x, g):
    xf = x.astype(jnp.float32)
    y = xf * lax.rsqrt(jnp.mean(xf * xf, axis=-1, keepdims=True) + EPS)
    return (y * g.astype(jnp.float32)).astype(x.dtype)

def _swiglu(h, w_gate_up, w_down):
    g, u = jnp.split(h @ w_gate_up, 2, axis=-1)
    return (jax.nn.silu(g) * u) @ w_down

def _memory_attention(q, mem_n, w_kv, q_g, k_g):
    b, s = q.shape[:2]
    m = mem_n.shape[1]
    q = _rmsnorm(q.reshape(b, s, MEM_HEADS, MEM_HEAD_DIM), q_g)
    k, v = jnp.split(mem_n @ w_kv, 2, axis=-1)
    k = _rmsnorm(k.reshape(b, m, MEM_HEADS, MEM_HEAD_DIM), k_g)
    v = v.reshape(b, m, MEM_HEADS, MEM_HEAD_DIM)
    scores = jnp.einsum("bshd,bmhd->bhsm", q, k).astype(jnp.float32) * (MEM_HEAD_DIM ** -0.5)
    p = jax.nn.softmax(scores, axis=-1).astype(v.dtype)
    o = jnp.einsum("bhsm,bmhd->bshd", p, v)
    return o.reshape(b, s, MEM_WIDTH)

def _causal_depthwise_conv(u, w, bias):
    c = u.shape[-1]
    out = lax.conv_general_dilated(
        u, w[:, None, :].astype(u.dtype), window_strides=(1,),
        padding=[(SSD_CONV - 1, 0)], dimension_numbers=("NWC", "WIO", "NWC"),
        feature_group_count=c)
    return out + bias

def _ssd_chunked(xs, dt, a, bm, cm):
    b, s = xs.shape[:2]
    nc = s // SSD_CHUNK
    L, G, R, P, N = SSD_CHUNK, SSD_GROUPS, SSD_HEADS_PER_GROUP, SSD_HEAD_DIM, SSD_STATE
    f32 = jnp.float32
    xdt = (xs.astype(f32) * dt[..., None]).reshape(b, nc, L, G, R, P)
    da = (dt * a).reshape(b, nc, L, G, R)
    bm = bm.astype(f32).reshape(b, nc, L, G, N)
    cm = cm.astype(f32).reshape(b, nc, L, G, N)
    cs = jnp.cumsum(da, axis=2)
    causal = jnp.tril(jnp.ones((L, L), dtype=bool))[:, :, None, None]
    seg = jnp.where(causal, cs[:, :, :, None] - cs[:, :, None, :], -jnp.inf)
    w_intra = jnp.einsum("bclgn,bcsgn->bclsg", cm, bm)[..., None] * jnp.exp(seg)
    y_diag = jnp.einsum("bclsgr,bcsgrp->bclgrp", w_intra, xdt)
    decay_to_end = jnp.exp(cs[:, :, -1:] - cs)
    chunk_states = jnp.einsum("bclgn,bclgr,bclgrp->bcgrpn", bm, decay_to_end, xdt)
    chunk_decay = jnp.exp(cs[:, :, -1])

    def step(state, inp):
        st, dec = inp
        return state * dec[..., None, None] + st, state

    h0 = jnp.zeros((b, G, R, P, N), f32)
    _, h_in = lax.scan(step, h0, (jnp.moveaxis(chunk_states, 1, 0), jnp.moveaxis(chunk_decay, 1, 0)))
    h_in = jnp.moveaxis(h_in, 0, 1)
    y_off = jnp.einsum("bclgn,bcgrpn->bclgrp", cm, h_in) * jnp.exp(cs)[..., None]
    return (y_diag + y_off).reshape(b, s, SSD_HEADS, P)

def _ssd_mix(h, mem_n, w_in, conv_w, conv_b, dt_bias, a_log, d_skip, norm_g, w_out,
             mem_w_kv, mq_g, mk_g):
    b, s, _ = h.shape
    proj = h @ w_in
    z, xbc, dt_raw, q_mem = jnp.split(
        proj, [SSD_INNER, SSD_INNER + SSD_CONV_DIM, SSD_INNER + SSD_CONV_DIM + SSD_HEADS], axis=-1)
    xbc = jax.nn.silu(_causal_depthwise_conv(xbc, conv_w, conv_b))
    xs, bm, cm = jnp.split(xbc, [SSD_INNER, SSD_INNER + SSD_GROUPS * SSD_STATE], axis=-1)
    dt = jax.nn.softplus(dt_raw.astype(jnp.float32) + dt_bias.astype(jnp.float32))
    a = -jnp.exp(a_log.astype(jnp.float32))
    xs = xs.reshape(b, s, SSD_HEADS, SSD_HEAD_DIM)
    y = _ssd_chunked(xs, dt, a,
                     bm.reshape(b, s, SSD_GROUPS, SSD_STATE),
                     cm.reshape(b, s, SSD_GROUPS, SSD_STATE))
    y = y + d_skip.astype(jnp.float32)[:, None] * xs.astype(jnp.float32)
    y = y.reshape(b, s, SSD_INNER) * jax.nn.silu(z.astype(jnp.float32))
    gs = SSD_INNER // SSD_GROUPS
    y = _rmsnorm(y.reshape(b, s, SSD_GROUPS, gs), norm_g.reshape(SSD_GROUPS, gs))
    y = y.reshape(b, s, SSD_INNER).astype(h.dtype)
    o_mem = _memory_attention(q_mem, mem_n, mem_w_kv, mq_g, mk_g)
    return jnp.concatenate([y, o_mem], axis=-1) @ w_out

def _stick_breaking(q, k, v):
    seq = q.shape[1]
    scale = SB_HEAD_DIM ** -0.5
    outs = []
    for blk in range(seq // SB_BLOCK):
        t0 = blk * SB_BLOCK
        end = t0 + SB_BLOCK
        qb, kb, vb = q[:, t0:end], k[:, :end], v[:, :end]
        z = jnp.einsum("bthd,bshd->bhts", qb, kb).astype(jnp.float32) * scale
        causal = jnp.arange(end)[None, :] < jnp.arange(t0, end)[:, None]
        log_1m = jnp.where(causal, jax.nn.log_sigmoid(-z), 0.0)
        log_survive = lax.cumsum(log_1m, axis=3, reverse=True) - log_1m
        w = jnp.where(causal, jnp.exp(jax.nn.log_sigmoid(z) + log_survive), 0.0)
        outs.append(jnp.einsum("bhts,bshd->bthd", w.astype(vb.dtype), vb))
    return jnp.concatenate(outs, axis=1)

def _sb_mix(h, mem_n, w_in, q_g, k_g, w_out, mem_w_kv, mq_g, mk_g):
    b, s, _ = h.shape
    q, k, v, q_mem = jnp.split(h @ w_in, [SB_WIDTH, 2 * SB_WIDTH, 3 * SB_WIDTH], axis=-1)
    shp = (b, s, SB_HEADS, SB_HEAD_DIM)
    q = _rmsnorm(q.reshape(shp), q_g)
    k = _rmsnorm(k.reshape(shp), k_g)
    o = _stick_breaking(q, k, v.reshape(shp)).reshape(b, s, SB_WIDTH)
    o_mem = _memory_attention(q_mem, mem_n, mem_w_kv, mq_g, mk_g)
    return jnp.concatenate([o, o_mem], axis=-1) @ w_out

def setup_inputs(seed: int = 0) -> dict:
    key = jax.random.key(seed)
    ks = jax.random.split(key, 24)
    nrm = jax.random.normal
    res_scale = 1.0 / math.sqrt(2 * DEPTH)
    dt = jnp.exp(jax.random.uniform(ks[10], (N_SSD_LAYERS, SSD_HEADS))
                 * (math.log(0.1) - math.log(0.001)) + math.log(0.001))
    return {
        "x": nrm(ks[0], (BATCH, SEQ, D_MODEL), jnp.float32),
        "mem": nrm(ks[1], (BATCH, MEM_LEN, D_MODEL), jnp.float32),
        "mix_norm_g": 1.0 + 0.02 * nrm(ks[2], (DEPTH, D_MODEL)),
        "ffn_norm_g": 1.0 + 0.02 * nrm(ks[3], (DEPTH, D_MODEL)),
        "mem_norm_g": 1.0 + 0.02 * nrm(ks[4], (D_MODEL,)),
        "mem_w_kv": nrm(ks[5], (DEPTH, D_MODEL, 2 * MEM_WIDTH)) * D_MODEL ** -0.5,
        "mem_q_norm_g": 1.0 + 0.02 * nrm(ks[6], (DEPTH, MEM_HEAD_DIM)),
        "mem_k_norm_g": 1.0 + 0.02 * nrm(ks[7], (DEPTH, MEM_HEAD_DIM)),
        "ssd_w_in": nrm(ks[8], (N_SSD_LAYERS, D_MODEL, SSD_IN)) * D_MODEL ** -0.5,
        "ssd_conv_w": nrm(ks[9], (N_SSD_LAYERS, SSD_CONV, SSD_CONV_DIM)) * SSD_CONV ** -0.5,
        "ssd_conv_b": 0.02 * nrm(ks[11], (N_SSD_LAYERS, SSD_CONV_DIM)),
        "ssd_dt_bias": dt + jnp.log(-jnp.expm1(-dt)),
        "ssd_a_log": jnp.log(jax.random.uniform(ks[12], (N_SSD_LAYERS, SSD_HEADS), minval=1.0, maxval=16.0)),
        "ssd_d": 1.0 + 0.02 * nrm(ks[13], (N_SSD_LAYERS, SSD_HEADS)),
        "ssd_norm_g": 1.0 + 0.02 * nrm(ks[14], (N_SSD_LAYERS, SSD_INNER)),
        "ssd_w_out": nrm(ks[15], (N_SSD_LAYERS, MIX_WIDTH, D_MODEL)) * MIX_WIDTH ** -0.5 * res_scale,
        "sb_w_in": nrm(ks[16], (N_SB_LAYERS, D_MODEL, SB_IN)) * D_MODEL ** -0.5,
        "sb_q_norm_g": 1.0 + 0.02 * nrm(ks[17], (N_SB_LAYERS, SB_HEAD_DIM)),
        "sb_k_norm_g": 1.0 + 0.02 * nrm(ks[18], (N_SB_LAYERS, SB_HEAD_DIM)),
        "sb_w_out": nrm(ks[19], (N_SB_LAYERS, MIX_WIDTH, D_MODEL)) * MIX_WIDTH ** -0.5 * res_scale,
        "ffn_w_gate_up": nrm(ks[20], (DEPTH, D_MODEL, 2 * FFN_HIDDEN)) * D_MODEL ** -0.5,
        "ffn_w_down": nrm(ks[21], (DEPTH, FFN_HIDDEN, D_MODEL)) * FFN_HIDDEN ** -0.5 * res_scale,
    }

def reference(x, mem, mix_norm_g, ffn_norm_g, mem_norm_g, mem_w_kv, mem_q_norm_g, mem_k_norm_g,
              ssd_w_in, ssd_conv_w, ssd_conv_b, ssd_dt_bias, ssd_a_log, ssd_d, ssd_norm_g, ssd_w_out,
              sb_w_in, sb_q_norm_g, sb_k_norm_g, sb_w_out, ffn_w_gate_up, ffn_w_down):
    mem_n = _rmsnorm(mem, mem_norm_g)
    for i in range(DEPTH):
        j = i // N_MIXERS
        h = _rmsnorm(x, mix_norm_g[i])
        if i % N_MIXERS == 0:
            mix = _ssd_mix(h, mem_n, ssd_w_in[j], ssd_conv_w[j], ssd_conv_b[j], ssd_dt_bias[j],
                           ssd_a_log[j], ssd_d[j], ssd_norm_g[j], ssd_w_out[j],
                           mem_w_kv[i], mem_q_norm_g[i], mem_k_norm_g[i])
        else:
            mix = _sb_mix(h, mem_n, sb_w_in[j], sb_q_norm_g[j], sb_k_norm_g[j], sb_w_out[j],
                          mem_w_kv[i], mem_q_norm_g[i], mem_k_norm_g[i])
        x = x + mix
        x = x + _swiglu(_rmsnorm(x, ffn_norm_g[i]), ffn_w_gate_up[i], ffn_w_down[i])
    return x


_drawn_inputs = setup_inputs


def setup_inputs(seed=0):
    import zlib

    import numpy as np

    out = dict(_drawn_inputs(seed))
    spreads = {}
    factors = {'mix_norm_g': 3.895,
     'ffn_norm_g': 5.524,
     'mem_norm_g': 8.0,
     'mem_q_norm_g': 8.0,
     'mem_k_norm_g': 8.0,
     'ssd_conv_b': 4.892,
     'ssd_d': 180.96,
     'ssd_norm_g': 6.254,
     'sb_q_norm_g': 93.487,
     'sb_k_norm_g': 35.147}
    for name, (base, spread) in spreads.items():
        noise = np.random.default_rng([zlib.crc32(name.encode()), seed]).standard_normal(out[name].shape)
        drawn = base * np.exp(spread * noise) if base else spread * noise
        out[name] = __import__('jax').numpy.asarray(drawn.astype(out[name].dtype))
    for name, factor in factors.items():
        out[name] = (out[name] * factor).astype(out[name].dtype)
    return out
```

```python
from contextlib import ExitStack

import concourse.bass as bass
from concourse import mybir

P = 128
SEQ, D, MEM = 256, 1024, 256
TOK = SEQ // P
KT = D // P
MIX = 2 * D
MEM_W = MIX // 4
MEM_HEADS = 4
INNER = MIX - MEM_W
GROUPS, STATE, HP = 4, 128, 64
HEADS = INNER // HP
HPG = HEADS // GROUPS
GW = INNER // GROUPS
CONV = 4
CONV_DIM = INNER + 2 * GROUPS * STATE
SB_HEADS = INNER // P
FFN = ((-(-8 * D // 3) + 255) // 256) * 256
EPS = 1e-6
FT = CONV_DIM // P
MT = MIX // P
HT = FFN // P
SCALE = float(P) ** -0.5

RING = 4
COLS = 512
UNIT_KT = 4

QM0 = INNER + CONV_DIM
DTQ = (HEADS + MEM_W) // 2
XB = INNER
IN0 = [("dtq0", QM0, DTQ), ("dtq1", QM0 + DTQ, DTQ),
       ("B", XB + INNER, COLS), ("C", XB + INNER + COLS, COLS),
       ("xs0", XB, COLS), ("xs1", XB + COLS, COLS), ("xs2", XB + 2 * COLS, COLS),
       ("km0", 0, COLS), ("vm0", MEM_W, COLS), ("km1", 0, COLS), ("vm1", MEM_W, COLS),
       ("z0", 0, COLS), ("z1", COLS, COLS), ("z2", 2 * COLS, COLS)]
IN1 = [("qm1", 3 * INNER, COLS)] + [(f"k{j}", INNER + j * COLS, COLS) for j in range(3)] + \
      [b for j in range(3) for b in ((f"q{j}", j * COLS, COLS), (f"v{j}", 2 * INNER + j * COLS, COLS))]
FFN_BLOCKS = FFN // 256
OUT0_ROWS = [12, 14, 0, 2, 4, 6, 8, 10]
OUT1_ROWS = [0, 2, 4, 6, 8, 10, 12, 14]
DOWN_ROWS = list(range(0, HT, 2))

U_IN0 = 0
U_OUT0 = U_IN0 + 2 * len(IN0)
U_FFN0 = U_OUT0 + len(OUT0_ROWS)
U_DOWN0 = U_FFN0 + 2 * FFN_BLOCKS
U_IN1 = U_DOWN0 + len(DOWN_ROWS)
U_OUT1 = U_IN1 + 2 * len(IN1)
U_FFN1 = U_OUT1 + len(OUT1_ROWS)
U_DOWN1 = U_FFN1 + 2 * FFN_BLOCKS
UNITS = U_DOWN1 + len(DOWN_ROWS)

A_IN0 = 0
A_OUT0 = A_IN0 + len(IN0)
A_FFN0 = A_OUT0 + 2
A_DOWN0 = A_FFN0 + FFN_BLOCKS
A_IN1 = A_DOWN0 + 2
A_OUT1 = A_IN1 + len(IN1)
A_FFN1 = A_OUT1 + 2
A_DOWN1 = A_FFN1 + FFN_BLOCKS

PLAN = {u: [] for u in range(-1, UNITS)}


def _plan():
    def at(u, *steps):
        PLAN[u] += steps

    def block_end(name):
        names = [n for n, _, _ in IN0]
        if name in names:
            return U_IN0 + 2 * names.index(name) + 1
        return U_IN1 + 2 * [n for n, _, _ in IN1].index(name) + 1

    def input_transposes(u, p):
        at(u, *[("xT", p, t, h) for t in range(TOK) for h in range(2)])

    at(-1, ("par", 0))
    input_transposes(-1, 0)
    at(1, ("par", 1))
    at(3, ("cs",))
    at(5, ("hT", "qm0", 0), ("hT", "qm0", 1))
    at(6, ("xb", 0, 0), ("xb", 0, 1))
    at(7, ("memT", 0, 0), ("memT", 0, 1))
    at(8, ("xb", 1, 0), ("xb", 1, 1))
    at(9, ("memT", 1, 0), ("memT", 1, 1), ("Bn",))
    at(10, ("xb", 2, 0), ("xb", 2, 1))
    at(11, ("G", 0), ("G", 1))
    at(12, ("xsn", 0, 0), ("xsn", 0, 1), ("xb", 3, 0), ("xb", 3, 1))
    at(14, ("xsn", 1, 0), ("xsn", 1, 1), ("xb", 4, 0), ("xb", 4, 1))
    at(16, ("xsn", 2, 0), ("xsn", 2, 1))
    at(17, ("hT", "km0", 0), ("hT", "km0", 1))
    gc = [(g, c) for g in range(GROUPS) for c in range(TOK)]
    for i in range(len(gc) + 2):
        if i >= 2:
            g, c = gc[i - 2]
            at(17 + i, ("yd", g, c))
            at(17 + i, ("yo", g) if c else ("st", g))
        if i < len(gc):
            at(17 + i, ("csb", *gc[i], 0), ("csb", *gc[i], 1))
    at(21, ("hT", "km1", 0), ("hT", "km1", 1))

    def memory_attention(l, u_scores, u_p0, u_o0, u_p1, u_o1):
        for u, (hp, t) in zip(u_scores, [(0, 0), (0, 1), (1, 0), (1, 1)]):
            at(u, ("sc", l, hp, t))
        at(u_p0, ("pT", l, 0), ("pT", l, 1))
        at(u_o0, ("mo", l, 0))
        at(u_p1, ("pT", l, 2), ("pT", l, 3))
        at(u_o1, ("mo", l, 1))

    at(26, ("gate", 0))
    memory_attention(0, (22, 23, 24, 25), 26, 27, 27, 27)
    at(27, ("gate", 1))
    at(28, *[("yT", j) for j in range(3)])
    at(29, *[("yT", j) for j in range(3, 6)])
    input_transposes(U_FFN0 - 1, 1)
    for l, u in ((0, U_FFN0), (1, U_FFN1)):
        for j in range(FFN_BLOCKS):
            at(u + 2 * j + 2, ("ffnT", l, j))
    input_transposes(U_IN1 - 1, 2)
    for n in ("qm1", "k0", "k1", "k2", "q0", "q1", "q2"):
        at(block_end(n) + 2, ("hT", n, 0), ("hT", n, 1))
    u = block_end("v0") + 1
    late = []
    for p in range(SB_HEADS // 2):
        a, b = 2 * p, 2 * p + 1
        at(u, ("z", a), ("z", b))
        at(u + 1, ("C", a), ("C", b))
        late += [(u + 2, ("O", a), ("O", b))]
        u += 2
    for step in late:
        at(*step)
    e = block_end("q2")
    memory_attention(1, (e - 5, e - 3, e - 1, e + 1), e + 3, e + 4, e + 4, e + 5)
    input_transposes(U_FFN1 - 1, 3)


_plan()

NO_BANK = ("gate",)
USES = {s: i for i, s in enumerate(s for u in sorted(PLAN) for s in PLAN[u] if s[0] not in NO_BANK)}
NAT = {"qm0": ("hT", "qm0", 1), "B": ("xb", 0, 1), "C": ("xb", 1, 1), "xs0": ("xb", 2, 1),
       "xs1": ("xb", 3, 1), "xs2": ("xb", 4, 1), "km0": ("hT", "km0", 1), "km1": ("hT", "km1", 1)}
NAT.update({n: ("hT", n, 1) for n in ("qm1", "k0", "k1", "k2", "q0", "q1", "q2")})
NAT_ORDER = list(NAT)
HEAD_NORMS = [n for n in NAT_ORDER if n[0] in "kq"]
CONV_TILES = [12, 16, 0, 4, 8]


def trunk(nc, x, mem, mix_norm_g, ffn_norm_g, mem_norm_g, mem_w_kv, mem_q_norm_g, mem_k_norm_g,
          ssd_w_in, ssd_conv_w, ssd_conv_b, ssd_dt_bias, ssd_a_log, ssd_d, ssd_norm_g, ssd_w_out,
          sb_w_in, sb_q_norm_g, sb_k_norm_g, sb_w_out, ffn_w_gate_up, ffn_w_down, out):
    F, R, I32 = mybir.dt.float32, mybir.dt.float32r, mybir.dt.int32
    ACT, ALU, AX = mybir.ActivationFunctionType, mybir.AluOpType, mybir.AxisListType

    ctx = ExitStack()
    with ctx:
        def sb(name, shape, dt=F):
            return ctx.enter_context(nc.sbuf_tensor(name, shape, dt))

        def under(specs):
            guards = [nc.sbuf_tensor(*s) for s in specs]
            made = [g.__enter__() for g in guards]
            for g in reversed(guards):
                g.__exit__(None, None, None)
            return made

        UW = UNIT_KT * COLS
        raw = under([(f"raw{i}", [P, UW], F) for i in range(RING)])
        lo = [sb(f"lo{i}", [P, UW], R) for i in range(RING)]
        hi = [sb(f"hi{i}", [P, UW], R) for i in range(RING)]
        aT_hi = sb("aT_hi", [P, KT, SEQ], R)
        aT_lo = sb("aT_lo", [P, KT, SEQ], R)
        xr = sb("xr", [P, TOK, D])
        nat = [sb(f"nat{i}", [P, TOK, COLS]) for i in range(2)]
        sq = sb("sq", [P, D])
        hg = [sb(f"hg{i}", [P, 4, P]) for i in range(2)]
        ident = sb("ident", [P, P])
        tle = sb("tle", [P, P])
        tlt = sb("tlt", [P, P])
        tgt = sb("tgt", [P, P])
        ones = sb("ones", [P, P])
        ROWS_A, ROWS_B = 80 + 20 + 8, 16 + 12 + 6
        vrow = sb("vrow", [P, 3, P])
        vcol = sb("vcol", [P, ROWS_A + ROWS_B + 16])
        kmT = [sb(f"kmT{l}", [P, MEM_HEADS, MEM]) for l in range(2)]
        vm = [sb(f"vm{l}", [P, 2, MEM_W]) for l in range(2)]
        small = sb("small", [P, 480])
        taken = [0]

        def cols(n):
            taken[0] += n
            return small[:, taken[0] - n:taken[0]]

        bias_b, alog_b, d_b = cols(HEADS), cols(HEADS), cols(HEADS)
        dtv, dta, dt = cols(2 * HEADS), cols(2 * HEADS), cols(2 * HEADS)
        da, cs, ecs, dte = cols(2 * HEADS), cols(2 * HEADS), cols(HEADS), cols(HEADS)
        ssq_x, rstd_x = cols(2), [cols(2) for _ in range(5)]
        ssq8, r8, v8, h8, t8 = cols(8), cols(8), cols(8), cols(8), cols(8)
        ssqy, ry = cols(8), cols(8)
        mx, sums, rsum = cols(2), cols(8), cols(2)
        gq_scaled = cols(1)

        oT_hi1, oT_lo1, qT, kT, vn, abuf, lsb, spb = under(
            [("oT_hi1", [P, MT, SEQ], R), ("oT_lo1", [P, MT, SEQ], R),
             ("qT", [P, SB_HEADS, SEQ], F), ("kT", [P, SB_HEADS, SEQ], F),
             ("vn", [P, 2, INNER], F), ("abuf", [P, 2, 384], F), ("lsb", [P, 4, 384], F),
             ("spb", [P, 2, 384], F)])
        uT_hi, uT_lo, sg, un = under(
            [("uT_hi", [P, HT, SEQ], R), ("uT_lo", [P, HT, SEQ], R),
             ("sg", [P, 2, TOK, 256], F), ("un", [P, 2, TOK, 256], F)])
        bcT, xsT, bn, gm, xpad, xdte, seg = under(
            [("bcT", [P, 8, SEQ], F), ("xsT", [P, 4, SEQ], F), ("bn", [P, 4, P], F),
             ("gm", [P, GROUPS, 2, P], F), ("xpad", [P, 2, HPG, P], F), ("xdte", [P, GW], F),
             ("seg", [P, 2, HPG, P], F)])
        oT_hi0 = sb("oT_hi0", [P, MT, SEQ], R)
        oT_lo0 = sb("oT_lo0", [P, MT, SEQ], R)
        y = sb("y", [P, TOK, INNER])
        zs = sb("zs", [P, TOK, INNER])
        conv = [zs[:, i, D:D + 512].rearrange("p (q t) -> p q t", q=2) for i in range(2)]
        p0, pT0 = under([("p0", [P, 2 * TOK, 2, MEM], F), ("pT0", [P, 2, 2, SEQ], F)])
        mT_hi = sb("mT_hi", [P, KT, SEQ], R)
        mT_lo = sb("mT_lo", [P, KT, SEQ], R)
        qmT0 = sb("qmT0", [P, MEM_HEADS, SEQ])
        state = sb("state", [P, GW])
        yoff = sb("yoff", [P, GW])
        memn = zs[:, :, 0:D]
        oT_hi, oT_lo = (oT_hi0, oT_hi1), (oT_lo0, oT_lo1)
        pm = ([p0[:, i] for i in range(4)],
              [b.rearrange("p a (b m) -> p (a b) m", m=MEM)[:, 2 * i:2 * i + 2, :] for b in (kmT[0][:], vm[0][:])
               for i in range(2)])
        pmT = (pT0[:], sq[:].rearrange("p (h m t) -> p h m t", h=2, m=2))

        def qmT(l, h):
            return qmT0[:, h:h + 2, :] if l == 0 else hg[h // 2][:].rearrange("p (a b) t -> p a (b t)", a=2)

        acc = [[ctx.enter_context(nc.psum_tensor(f"acc{i}{j}", [P, COLS], F)) for j in range(2)]
               for i in range(2)]
        bank = [ctx.enter_context(nc.psum_tensor(f"bank{i}", [P, COLS], F)) for i in range(4)]

        sems = {}

        def S(name):
            if name not in sems:
                sems[name] = ctx.enter_context(nc.semaphore(name))
            return sems[name]

        raw_landed = [S(f"raw_landed{i}") for i in range(RING)]
        hi_ready, lo_ready, unit_used = S("hi_ready"), S("lo_ready"), S("unit_used")
        acc_done = S("acc_done")
        acc_free = [S(f"acc_free{i}") for i in range(2)]
        bank_full = [S(f"bank_full{i}") for i in range(4)]
        bank_read = [S(f"bank_read{i}") for i in range(4)]

        def col_unit(w, c0, width, half):
            rows = w[half * UNIT_KT * P:(half + 1) * UNIT_KT * P, c0:c0 + width]
            return rows.rearrange("(t p) n -> p t n", p=P)

        def gate_up_unit(l, j, half):
            return [col_unit(ffn_w_gate_up[l], g * FFN + j * 256, 256, half) for g in range(2)]

        def row_unit(w, kt):
            return w[kt * P:(kt + 2) * P, :].rearrange("(t p) n -> p t n", p=P)

        SRC = []
        for name, c0, width in IN0:
            w = mem_w_kv[int(name[2])] if name[1:2] == "m" else ssd_w_in[0]
            SRC += [(col_unit(w, c0, width, h), UNIT_KT * width) for h in range(2)]
        SRC += [(row_unit(ssd_w_out[0], kt), UW) for kt in OUT0_ROWS]
        SRC += [(gate_up_unit(0, j, h), UW) for j in range(FFN_BLOCKS) for h in range(2)]
        SRC += [(row_unit(ffn_w_down[0], kt), UW) for kt in DOWN_ROWS]
        SRC += [(col_unit(sb_w_in[0], c0, w_, h), UNIT_KT * w_) for _, c0, w_ in IN1 for h in range(2)]
        SRC += [(row_unit(sb_w_out[0], kt), UW) for kt in OUT1_ROWS]
        SRC += [(gate_up_unit(1, j, h), UW) for j in range(FFN_BLOCKS) for h in range(2)]
        SRC += [(row_unit(ffn_w_down[1], kt), UW) for kt in DOWN_ROWS]

        LANDED = []
        for u, (src, _) in enumerate(SRC):
            LANDED.append((LANDED[u - RING] if u >= RING else 0) + 16 * (2 if isinstance(src, list) else 1))

        ENDS = {}
        for i, (name, _, width) in enumerate(IN0):
            ENDS[U_IN0 + 2 * i + 1] = ("block", A_IN0 + i, name, width)
        for i, (name, _, width) in enumerate(IN1):
            ENDS[U_IN1 + 2 * i + 1] = ("block", A_IN1 + i, name, width)
        for l, (u, a) in enumerate(((U_FFN0, A_FFN0), (U_FFN1, A_FFN1))):
            for j in range(FFN_BLOCKS):
                ENDS[u + 2 * j + 1] = ("ffn", a + j, l, j)
        for i, (u, a) in enumerate(((U_FFN0, A_OUT0), (U_IN1, A_DOWN0), (U_FFN1, A_OUT1), (UNITS, A_DOWN1))):
            ENDS[u - 1] = ("rows", a, i)

        done_before, total = {}, 0
        for u in sorted(ENDS):
            kind, a = ENDS[u][:2]
            done_before[a] = total
            total += 3 if kind == "rows" else 1

        def wait_acc(eng, u, j, rows_j=None):
            kind, a = ENDS[u][:2]
            if j == (3 if kind == "rows" else 1):
                eng.wait_ge(unit_used, u + 1)
            else:
                eng.wait_ge(acc_done, done_before[a] + j + 1)

        ROWS_AT = [A_OUT0, A_DOWN0, A_OUT1, A_DOWN1]
        MODE = {}
        for i, a0 in enumerate(ROWS_AT):
            for t in range(TOK):
                MODE[a0 + t] = ("rows", i, t)
        col_free = {}
        n_col = [0, 0]
        for a in range(A_DOWN1 + 2):
            if a not in MODE:
                n_col[a % 2] += TOK
            col_free[a] = n_col[a % 2]

        def wait_acc_read(eng, a, j):
            eng.wait_ge(acc_free[a % 2], col_free[a] - TOK + j + 1)

        def T(step):
            return bank[USES[step] % 4]

        def wait_full(eng, step):
            eng.wait_ge(bank_full[USES[step] % 4], USES[step] // 4 + 1)

        def wait_read(eng, step):
            eng.wait_ge(bank_read[USES[step] % 4], USES[step] // 4 + 1)

        def filled(step, ins):
            ins.then_inc(bank_full[USES[step] % 4], 1)

        def read(step, ins):
            ins.then_inc(bank_read[USES[step] % 4], 1)

        BLOCK_ACC = {n: A_IN0 + i for i, (n, _, _) in enumerate(IN0)}
        BLOCK_ACC.update({n: A_IN1 + i for i, (n, _, _) in enumerate(IN1)})

        def natb(name):
            return nat[NAT_ORDER.index(name) % 2]

        def each(ap, n):
            return ap.unsqueeze(2).broadcast_to([P, ap.shape[1], n])

        def whole(ap, k):
            return ap.unsqueeze(1).broadcast_to([P, k, ap.shape[1]])

        def heads_of(c, g, n=HPG, first=0):
            at = c * HEADS + g * HPG + first
            return slice(at, at + n)

        def conv_w(j, ft):
            return vcol[:, j * FT + ft:j * FT + ft + 1]

        def conv_b(ft):
            return vcol[:, 80 + ft:81 + ft]

        MIX_G = ROWS_A + ROWS_B
        XT_GAIN = [MIX_G, ROWS_A, MIX_G + KT, ROWS_A + KT, 100]
        NORM_G = ROWS_A + 16
        MQ, MK, SQ_, SK_ = ROWS_A + 28, ROWS_A + 30, ROWS_A + 32, ROWS_A + 33

        def xt_index(step):
            if step[0] == "memT":
                return 4 + 2 * step[1] + step[2]
            _, p, t, h = step
            return (0 if p == 0 else 4 + 4 * p) + 2 * t + h

        SC_ORDER = [(l, hp, t) for l in range(2) for hp in range(2) for t in range(TOK)]

        block = ctx.enter_context(nc.Block())

        @block.sync
        def _(sp):
            for u in range(UNITS):
                src, n = SRC[u]
                if u >= RING:
                    sp.wait_ge(unit_used, u - RING + 1)
                srcs = src if isinstance(src, list) else [src]
                dst = raw[u % RING][:, 0:n].rearrange("p (t g n) -> p t g n", t=srcs[0].shape[1], g=len(srcs))
                for g, part in enumerate(srcs):
                    sp.dma_start(dst[:, :, g, :], part).then_inc(raw_landed[u % RING], 16)

        @block.gpsimd
        def _(pool):
            made = [0]

            def link(ins):
                made[0] += 1
                ins.then_inc(S("pool_seq"), 1)
                pool.wait_ge(S("pool_seq"), made[0])

            link(nc.gpsimd.memset(ones[:], 1.0))
            for m, op, cm, step in ((ident, ALU.is_equal, 1, -1), (tle, ALU.is_ge, -1, 1),
                                    (tlt, ALU.is_gt, -1, 1), (tgt, ALU.is_gt, 1, -1)):
                nc.gpsimd.affine_select(out=m[:], in_=ones[:], compare_op=op, fill=0.0, base=0,
                                        pattern=[[step, P]], channel_multiplier=cm).then_inc(S("masks"), 1)
            nc.gpsimd.memset(xpad[:].rearrange("p c h n -> p (c h n)"), 0.0).then_inc(S("xpad_clear"), 1)
            pool.wait_ge(S("xpad_clear"), 1)

            def scan_inputs(g, c):
                if g == 0 and c == 0:
                    for j in range(3):
                        for t in range(TOK):
                            wait_read(pool, ("xsn", j, t))
                    pool.wait_ge(S("dtdte"), 1)
                if g:
                    wait_full(pool, ("yd", g - 1, c))
                xg = y[:, c, g * GW:(g + 1) * GW].rearrange("p (j e n) -> p j e n", e=2, n=HP)
                xp = xpad[:, c].rearrange("p (j e) n -> p j e n", e=2)
                dg = dt[:, heads_of(c, g)].rearrange("p (j e) -> p j e", e=2)
                for e in range(2):
                    last = nc.gpsimd.tensor_tensor(xp[:, :, e, e * HP:(e + 1) * HP], xg[:, :, e, :],
                                                   each(dg[:, :, e], HP), ALU.mult)
                last.then_inc(S("xpad"), 1)
                if c == 0:
                    if g:
                        wait_full(pool, ("st", g - 1))
                    nc.gpsimd.tensor_tensor(xdte[:].rearrange("p (h n) -> p h n", n=HP),
                                            y[:, 0, g * GW:(g + 1) * GW].rearrange("p (h n) -> p h n", n=HP),
                                            each(dte[:, heads_of(0, g)], HP), ALU.mult).then_inc(S("xdte"), 1)
                pool.wait_ge(S("xpad"), 2 * g + c + 1)
                pool.wait_ge(S("xdte"), g + 1)
                yg = y[:, c, g * GW:(g + 1) * GW].rearrange("p (h n) -> p h n", n=HP)
                nc.gpsimd.tensor_tensor(yg, yg, each(d_b[:, heads_of(0, g)], HP), ALU.mult).then_inc(S("skip"), 1)

            def diag_mask(buf, s):
                v = buf[:, s].rearrange("p (b t) -> p b t", t=P)[:, 0:3:2, :]
                return nc.gpsimd.tensor_tensor(v, v, whole(tlt[:], 2), ALU.mult)

            for u in range(-1, UNITS):
                for step in PLAN[u]:
                    kind = step[0]
                    if kind == "csb" and step[3] == 0:
                        scan_inputs(step[1], step[2])
                    elif kind == "yo":
                        g = step[1]
                        wait_read(pool, ("yd", g, 1))
                        wait_read(pool, step)
                        yg = y[:, 1, g * GW:(g + 1) * GW]
                        nc.gpsimd.tensor_tensor(yg, yg, yoff[:], ALU.add).then_inc(S("y_whole"), 1)
                    elif kind == "z":
                        wait_read(pool, step)
                        diag_mask(spb, step[1] % 2).then_inc(S("sp_masked"), 1)
                    elif kind == "C":
                        pool.wait_ge(S("w_exp"), step[1] + 1)
                        diag_mask(lsb, step[1] % 4).then_inc(S("w_masked"), 1)

        @block.scalar
        def _(act):
            made = [0]

            def link(ins):
                made[0] += 1
                ins.then_inc(S("act_seq"), 1)
                act.wait_ge(S("act_seq"), made[0])

            def f(out_, in_, func=ACT.Copy, **k):
                return nc.scalar.activation(out_, in_, func, **k)

            act.dma_start(vrow[0:16, 2, :], mix_norm_g.rearrange("l (f p) -> (l f) p", p=P)).then_inc(S("gain_landed"), 16)
            for t in range(TOK):
                act.dma_start(xr[:, t, :], x[0, t * P:(t + 1) * P, :]).then_inc(S(f"x_landed{t}"), 16)
            rows = [(0, 0, ssd_conv_w[0].rearrange("j (f p) -> (j f) p", p=P)),
                    (0, 80, ssd_conv_b[0].rearrange("(f p) -> f p", p=P)),
                    (0, 100, mem_norm_g.rearrange("(f p) -> f p", p=P)),
                    (1, 0, ffn_norm_g.rearrange("l (f p) -> (l f) p", p=P)),
                    (1, 16, ssd_norm_g[0].rearrange("(f p) -> f p", p=P)),
                    (1, 28, mem_q_norm_g), (1, 30, mem_k_norm_g), (1, 32, sb_q_norm_g), (1, 33, sb_k_norm_g)]
            act.preload_act_table_set("natural_log_exp_and_others")
            for b, r, v in rows:
                act.dma_start(vrow[r:r + v.shape[0], b, :], v).then_inc(S("vectors_landed"), 16)
            for dst, v in ((bias_b, ssd_dt_bias), (alog_b, ssd_a_log), (d_b, ssd_d)):
                act.dma_start(dst, v.broadcast_to([P, HEADS])).then_inc(S("head_vectors_landed"), 16)
            for t in range(TOK):
                act.dma_start(memn[:, t, :], mem[0, t * P:(t + 1) * P, :]).then_inc(S("mem_landed"), 16)

            split_at = [0]

            def split_to(u):
                while split_at[0] < min(u, UNITS):
                    v = split_at[0]
                    n = SRC[v][1]
                    act.wait_ge(raw_landed[v % RING], LANDED[v])
                    f(hi[v % RING][:, 0:n], raw[v % RING][:, 0:n]).then_inc(hi_ready, 1)
                    split_at[0] += 1

            ssq_sums = [0]

            def sum_squares(p, src):
                i = ssq_sums[0]
                for t in range(TOK):
                    f(sq[:], src[:, t, :], ACT.Square, accum_out=ssq_x[:, t:t + 1]).then_inc(S("x_ssq"), 1)
                    act.wait_ge(S("x_ssq"), TOK * i + t + 1)
                ssq_sums[0] += 1

            def end_block(u, a, name, width):
                rs = rstd_x[4 if name[1:2] == "m" and name[0] in "kv" else (0 if u < U_OUT0 else 2)]
                if name == "dtq0":
                    act.wait_ge(S("rstd"), 1)
                if name == "km0":
                    act.wait_ge(S("rstd"), 2)
                if name == "qm1":
                    act.wait_ge(S("rstd"), 4)
                if name in NAT_ORDER and NAT_ORDER.index(name) >= 2:
                    wait_full(act, NAT[NAT_ORDER[NAT_ORDER.index(name) - 2]])
                for t in range(TOK):
                    wait_acc(act, u, t)
                    ps, r = acc[a % 2][t], rs[:, t:t + 1]
                    if name == "dtq0":
                        link(f(dtv[:, t * HEADS:(t + 1) * HEADS], ps[:, 0:HEADS], scale=r))
                        last = f(natb("qm0")[:, t, 0:width - HEADS], ps[:, HEADS:width], scale=r)
                    elif name == "dtq1":
                        last = f(natb("qm0")[:, t, DTQ - HEADS:MEM_W], ps[:, 0:width], scale=r)
                    elif name[0] == "z":
                        j = int(name[1])
                        last = f(zs[:, t, j * COLS:(j + 1) * COLS], ps[:], scale=r)
                    elif name[:2] == "vm":
                        last = f(vm[int(name[2])][:, t, :], ps[:], scale=r)
                    elif name[0] == "v":
                        j = int(name[1])
                        last = f(vn[:, t, j * COLS:(j + 1) * COLS], ps[:], scale=r)
                    else:
                        last = f(natb(name)[:, t, :], ps[:], scale=r)
                    last.then_inc(acc_free[a % 2], 1)
                name = "qm0" if name == "dtq1" else name
                if name in HEAD_NORMS:
                    i = HEAD_NORMS.index(name)
                    wait_acc_read(act, a, 1)
                    wait_acc_read(act, a - 1, 1)
                    if i:
                        act.wait_ge(S("nat_normed"), i)
                    f(sq[:], natb(name)[:].rearrange("p t n -> p (t n)"), ACT.Square).then_inc(S("squares"), 1)

            def dt_scan():
                act.wait_ge(S("dt_biased"), 1)
                link(f(dta, dtv, ACT.Abs))
                link(f(dta, dta, ACT.Exp, scale=-1.0))
                f(dta, dta, ACT.Ln, bias=1.0).then_inc(S("dt_log"), 1)
                act.wait_ge(S("head_vectors_landed"), 48)
                f(alog_b, alog_b, ACT.Exp).then_inc(S("dt_log"), 1)

            def step_xT(step):
                i = xt_index(step)
                mem_ = step[0] == "memT"
                t, h = step[-2:]
                dst = (mT_hi if mem_ else aT_hi)[:, 4 * h:4 * h + 4, t * P:(t + 1) * P]
                act.wait_ge(S("hg"), i + 1)
                f(dst, hg[i % 2][:]).then_inc(S("aT_hi"), 1)

            def conv_first(i, h):
                step, n = ("xb", i, h), 2 * i + h
                ft = CONV_TILES[i] + 2 * h
                wait_full(act, step)
                for q in range(2):
                    last = f(conv[n % 2][:, q, :], T(step)[:, q * SEQ:(q + 1) * SEQ], ACT.Identity,
                             scale=conv_w(3, ft + q), bias=conv_b(ft + q))
                last.then_inc(S("conv_first"), 1)

            def conv_silu(i, h):
                wait_read(act, ("xb", i, h))
                if i >= 3 and h == 0:
                    wait_full(act, ("xsn", i - 3, 1))
                dst = bcT[:, 4 * i + 2 * h:4 * i + 2 * h + 2, :] if i < 2 else xsT[:, 2 * h:2 * h + 2, :]
                f(dst, conv[h][:], ACT.Silu).then_inc(S("conv_silu"), 1)

            def steps(step):
                kind = step[0]
                if kind in ("xT", "memT"):
                    step_xT(step)
                elif kind == "cs":
                    wait_read(act, step)
                    f(dte, dte, ACT.Exp).then_inc(S("cs_exp"), 1)
                    f(ecs, cs[:, HEADS:2 * HEADS], ACT.Exp).then_inc(S("cs_exp"), 1)
                elif kind == "hT":
                    _, name, h = step
                    if name[:2] == "qm":
                        l = int(name[2])
                        dst, gain = qmT(l, 2 * h), vcol[:, MQ + l:MQ + l + 1]
                    elif name[:2] == "km":
                        l = int(name[2])
                        dst, gain = kmT[l][:, 2 * h:2 * h + 2, :], vcol[:, MK + l:MK + l + 1]
                    else:
                        base = 4 * int(name[1]) + 2 * h
                        dst = (qT if name[0] == "q" else kT)[:, base:base + 2, :]
                        gain = gq_scaled if name[0] == "q" else vcol[:, SK_:SK_ + 1]
                    wait_full(act, step)
                    read(step, f(dst.rearrange("p h t -> p (h t)"), T(step)[:], scale=gain))
                elif kind == "xb":
                    if step[2] == 0:
                        conv_first(step[1], 0)
                        conv_first(step[1], 1)
                    else:
                        conv_silu(step[1], 0)
                        conv_silu(step[1], 1)
                elif kind == "xsn":
                    _, j, t = step
                    wait_full(act, step)
                    read(step, f(y[:, t, j * COLS:(j + 1) * COLS], T(step)[:]))
                elif kind == "Bn":
                    wait_full(act, step)
                    read(step, f(bn[:].rearrange("p g n -> p (g n)"), T(step)[:]))
                elif kind == "csb" and step[3] == 1:
                    i = 2 * step[1] + step[2]
                    wait_read(act, ("csb", step[1], step[2], 0))
                    wait_read(act, step)
                    s = seg[:, i % 2].rearrange("p h l -> p (h l)")
                    f(s, s, ACT.Exp).then_inc(S("seg_exp"), 1)
                elif kind == "st":
                    g = step[1]
                    wait_full(act, step)
                    if g:
                        wait_full(act, ("yo", g - 1))
                    read(step, f(state[:], T(step)[:, 0:GW]))
                elif kind == "gate":
                    half = step[1]
                    s = slice(0, 2 * COLS) if half == 0 else slice(2 * COLS, INNER)
                    for t in range(TOK):
                        f(zs[:, t, s], zs[:, t, s], ACT.Silu).then_inc(S("z_silu"), 1)
                    for g in (2 * half, 2 * half + 1):
                        act.wait_ge(S("gated"), g + 1)
                        for t in range(TOK):
                            at = 4 * half + 2 * t + g % 2
                            f(sq[:, 0:GW], y[:, t, g * GW:(g + 1) * GW], ACT.Square,
                              accum_out=ssqy[:, at:at + 1]).then_inc(S("y_ssq"), 1)
                            act.wait_ge(S("y_ssq"), TOK * g + t + 1)
                elif kind == "yT":
                    j = step[1]
                    wait_full(act, step)
                    for q in range(2):
                        last = f(oT_hi0[:, 2 * j + q, :], T(step)[:, q * SEQ:(q + 1) * SEQ],
                                 scale=vcol[:, NORM_G + 2 * j + q:NORM_G + 2 * j + q + 1])
                    last.then_inc(S("yT_hi"), 1)
                elif kind == "sc":
                    _, l, hp, t = step
                    i = SC_ORDER.index((l, hp, t))
                    act.wait_ge(S("score_max"), i + 1)
                    for h in range(2):
                        k = 4 * t + 2 * hp + h
                        last = f(pm[l][2 * hp + t][:, h, :], T(step)[:, h * MEM:(h + 1) * MEM], ACT.Exp,
                                 scale=SCALE, bias=mx[:, h:h + 1], accum_out=sums[:, k:k + 1])
                        if h == 0:
                            link(last)
                    read(step, last)
                elif kind == "pT":
                    _, l, h = step
                    wait_full(act, step)
                    if h >= 2:
                        wait_full(act, ("mo", l, 0))
                    read(step, f(pmT[l][:, h % 2].rearrange("p m t -> p (m t)"), T(step)[:]))
                elif kind == "mo":
                    _, l, hp = step
                    wait_full(act, step)
                    f(oT_hi[l][:, 12 + 2 * hp:14 + 2 * hp, :].rearrange("p h t -> p (h t)"),
                      T(step)[:]).then_inc(S("mo_hi"), 1)
                elif kind == "ffnT":
                    _, l, j = step
                    wait_full(act, step)
                    f(uT_hi[:, 2 * j:2 * j + 2, :].rearrange("p k t -> p (k t)"), T(step)[:]).then_inc(S("uT_hi"), 1)
                elif kind == "z":
                    if step[1] == 0:
                        act.preload_act_table_set("natural_log_exp_and_others")
                    if step[1] % 2 == 0:
                        return
                    pair = (step[1] - 1, step[1])
                    for h in pair:
                        wait_full(act, ("z", h))
                        last = f(abuf[:, h % 2], T(("z", h))[:, 0:384], ACT.Abs)
                    link(last)
                    for h in pair:
                        last = f(abuf[:, h % 2], abuf[:, h % 2], ACT.Exp, scale=-1.0)
                    link(last)
                    for h in pair:
                        f(abuf[:, h % 2], abuf[:, h % 2], ACT.Ln, bias=1.0).then_inc(S("log1p"), 1)
                elif kind == "C":
                    b = lsb[:, step[1] % 4]
                    wait_read(act, step)
                    f(b, b, ACT.Exp).then_inc(S("w_exp"), 1)
                elif kind == "O":
                    wait_full(act, step)
                    f(oT_hi1[:, step[1], :], T(step)[:, 0:SEQ]).then_inc(S("O_hi"), 1)

            for u in range(-1, UNITS):
                if ("xT", 0, 0, 0) in PLAN[u] or u in ENDS and ENDS[u][0] == "rows":
                    if u == UNITS - 1:
                        break
                    for t in range(TOK):
                        split_to(u + 2 + t)
                        for step in PLAN[u]:
                            if step[0] == "xT" and step[2] == t:
                                steps(step)
                    if u == -1:
                        for t in range(TOK):
                            act.wait_ge(S(f"x_landed{t}"), 16)
                        sum_squares(0, xr)
                    else:
                        i = ENDS[u][2]
                        act.wait_ge(S("x_added"), 4 * (i + 1))
                        sum_squares(i + 1, xr)
                    if u in (U_FFN0 - 1, U_FFN1 - 1):
                        act.preload_act_table_set("silu_and_others")
                    continue
                split_to(u + 3)
                if u in ENDS:
                    kind, a = ENDS[u][:2]
                    if kind == "block":
                        end_block(u, a, *ENDS[u][2:])
                        if ENDS[u][2] == "dtq0":
                            dt_scan()
                    elif kind == "ffn":
                        l, j = ENDS[u][2:]
                        if j == 0:
                            act.wait_ge(S("rstd"), 3 + 2 * l)
                        for t in range(TOK):
                            wait_acc(act, u, t)
                            f(sg[:, j % 2, t, :], acc[a % 2][t][:, 0:256], ACT.Silu,
                              scale=rstd_x[2 * l + 1][:, t:t + 1]).then_inc(S("gate_silu"), 1)
                for step in PLAN[u]:
                    steps(step)
                if u == 9:
                    act.wait_ge(S("mem_landed"), 32)
                    act.wait_ge(S("nat_normed"), 1)
                    sum_squares(4, memn)
            for t in range(TOK):
                for h in range(2):
                    act.wait_ge(S("x_added"), 13 + 2 * t + h)
                    c = slice(h * COLS, (h + 1) * COLS)
                    act.dma_start(out[0, t * P:(t + 1) * P, c], xr[:, t, c]).then_inc(S("out_written"), 16)
            act.wait_ge(S("out_written"), 64)

        @block.vector
        def _(dve):
            made = [0]

            def link(ins):
                made[0] += 1
                ins.then_inc(S("dve_seq"), 1)
                dve.wait_ge(S("dve_seq"), made[0])

            v = nc.vector
            split_at = [0]

            def split_to(u):
                while split_at[0] < min(u, UNITS):
                    w = split_at[0]
                    n = SRC[w][1]
                    dve.wait_ge(hi_ready, w + 1)
                    v.tensor_tensor(lo[w % RING][:, 0:n], raw[w % RING][:, 0:n],
                                    hi[w % RING][:, 0:n].bitcast(F), ALU.subtract).then_inc(lo_ready, 1)
                    split_at[0] += 1

            def rsqrt(dst, ssq, n, count, done, nth):
                a, h, t = v8[:, 0:n], h8[:, 0:n], t8[:, 0:n]
                link(v.tensor_scalar(a, ssq, 1.0 / count, EPS, ALU.mult, ALU.add))
                link(v.tensor_scalar(t.bitcast(I32), a.bitcast(I32), 1, None, ALU.logical_shift_right))
                link(v.tensor_scalar(h, a, -0.5, None, ALU.mult))
                link(v.tensor_scalar(dst.bitcast(I32), t.bitcast(I32), -1.0, float(0x5f3759df), ALU.mult, ALU.add))
                for i in range(3):
                    link(v.tensor_tensor(t, dst, dst, ALU.mult))
                    link(v.tensor_tensor(t, t, h, ALU.mult))
                    last = v.scalar_tensor_tensor(dst, t, 1.5, dst, ALU.add, ALU.mult)
                    if i < 2:
                        link(last)
                last.then_inc(done, 1)
                dve.wait_ge(done, nth)

            def row_norm(p, i):
                dve.wait_ge(S("x_ssq"), TOK * i)
                rsqrt(rstd_x[p], ssq_x, 2, D, S("rstd"), i)

            def step_xT(step):
                i = xt_index(step)
                mem_ = step[0] == "memT"
                t, h = step[-2:]
                g0 = XT_GAIN[4 if mem_ else step[1]] + 4 * h
                wait_full(dve, step)
                b = hg[i % 2]
                v.tensor_tensor(b[:], T(step)[:].rearrange("p (k t) -> p k t", k=4),
                                each(vcol[:, g0:g0 + 4], P), ALU.mult).then_inc(S("hg"), 1)
                sl = (slice(None), slice(4 * h, 4 * h + 4), slice(t * P, (t + 1) * P))
                dve.wait_ge(S("aT_hi"), i + 1)
                read(step, v.tensor_tensor((mT_lo if mem_ else aT_lo)[sl], b[:],
                                           (mT_hi if mem_ else aT_hi)[sl].bitcast(F), ALU.subtract))

            def steps(step):
                kind = step[0]
                if kind == "par" and step[1] == 0:
                    wait_full(dve, step)
                    read(step, v.tensor_copy(vcol[:, MIX_G:MIX_G + 16], T(step)[:, 0:16]))
                    wait_read(dve, step)
                elif kind == "par":
                    wait_full(dve, step)
                    link(v.tensor_copy(vcol[:, 0:ROWS_A], T(step)[:, 0:ROWS_A]))
                    read(step, v.tensor_copy(vcol[:, ROWS_A:ROWS_A + ROWS_B], T(step)[:, P:P + ROWS_B]))
                    wait_read(dve, step)
                    link(v.tensor_scalar(gq_scaled, vcol[:, SQ_:SQ_ + 1], SCALE, None, ALU.mult))
                elif kind in ("xT", "memT"):
                    step_xT(step)
                elif kind == "cs":
                    wait_full(dve, step)
                    link(v.tensor_copy(cs, T(step)[:, 0:2 * HEADS]))
                    read(step, v.tensor_tensor(dte, T(step)[:, 2 * HEADS:3 * HEADS], cs[:, 0:HEADS], ALU.subtract))
                    dve.wait_ge(S("cs_exp"), 2)
                    v.tensor_tensor(dte, dte, dt[:, 0:HEADS], ALU.mult).then_inc(S("dtdte"), 1)
                elif kind == "xb":
                    _, i, h = step
                    n = 2 * i + h
                    ft = CONV_TILES[i] + 2 * h
                    dve.wait_ge(S("conv_first"), n + 1)
                    for tap in (1, 2, 3):
                        for q in range(2):
                            c_ = conv[n % 2][:, q, tap:SEQ]
                            last = v.scalar_tensor_tensor(c_, T(step)[:, q * SEQ:(q + 1) * SEQ - tap],
                                                          conv_w(3 - tap, ft + q), c_, ALU.mult, ALU.add)
                            if tap == 3 and q == 1:
                                read(step, last)
                            elif q == 1:
                                link(last)
                elif kind == "G":
                    wait_full(dve, step)
                    a = step[1]
                    read(step, v.tensor_tensor(gm[:, 2 * a:2 * a + 2].rearrange("p g c l -> p (g c) l"),
                                               T(step)[:].rearrange("p (k l) -> p k l", k=4),
                                               whole(tle[:], 4), ALU.mult))
                elif kind == "csb":
                    _, g, c, h = step
                    i = 2 * g + c
                    if i >= 2:
                        wait_full(dve, ("yd", (i - 2) // 2, i % 2))
                    wait_full(dve, step)
                    for q in range(3):
                        col = heads_of(c, g, 1, 3 * h + q)
                        last = v.tensor_scalar(seg[:, i % 2, 3 * h + q, :], T(step)[:, q * P:(q + 1) * P],
                                               cs[:, col], 0.0, ALU.subtract, ALU.min)
                    read(step, last)
                    if h == 1:
                        dve.wait_ge(S("seg_exp"), i + 1)
                        s = seg[:, i % 2]
                        v.tensor_tensor(s, s, whole(gm[:, g, c, :], HPG), ALU.mult).then_inc(S("w_scan"), 1)
                elif kind == "yd":
                    _, g, c = step
                    yg = y[:, c, g * GW:(g + 1) * GW]
                    wait_full(dve, step)
                    dve.wait_ge(S("skip"), 2 * g + c + 1)
                    read(step, v.tensor_tensor(yg, T(step)[:, 0:GW], yg, ALU.add))
                elif kind == "yo":
                    g = step[1]
                    wait_full(dve, step)
                    if g:
                        dve.wait_ge(S("y_whole"), g)
                    read(step, v.tensor_tensor(yoff[:].rearrange("p (h n) -> p h n", n=HP),
                                               T(step)[:, 0:GW].rearrange("p (h n) -> p h n", n=HP),
                                               each(ecs[:, heads_of(0, g)], HP), ALU.mult))
                elif kind == "hT":
                    pass
                elif kind == "gate":
                    half = step[1]
                    dve.wait_ge(S("z_silu"), TOK * (half + 1))
                    dve.wait_ge(S("y_whole"), 2 * half + 2)
                    for g in (2 * half, 2 * half + 1):
                        s = slice(g * GW, (g + 1) * GW)
                        v.tensor_tensor(y[:, :, s], y[:, :, s], zs[:, :, s], ALU.mult).then_inc(S("gated"), 1)
                    dve.wait_ge(S("y_ssq"), TOK * 2 * (half + 1))
                    ryh = ry[:, 4 * half:4 * half + 4]
                    rsqrt(ryh, ssqy[:, 4 * half:4 * half + 4], 4, GW, S("y_rstd"), half + 1)
                    for t in range(TOK):
                        yt = y[:, t, 2 * half * GW:2 * (half + 1) * GW].rearrange("p (g n) -> p g n", n=GW)
                        v.tensor_tensor(yt, yt, each(ryh[:, 2 * t:2 * t + 2], GW), ALU.mult).then_inc(S("y_normed"), 1)
                elif kind == "yT":
                    j = step[1]
                    dve.wait_ge(S("yT_hi"), j + 1)
                    for q in range(2):
                        g = NORM_G + 2 * j + q
                        last = v.scalar_tensor_tensor(oT_lo0[:, 2 * j + q, :], T(step)[:, q * SEQ:(q + 1) * SEQ],
                                                      vcol[:, g:g + 1], oT_hi0[:, 2 * j + q, :].bitcast(F),
                                                      ALU.mult, ALU.subtract)
                    read(step, last)
                elif kind == "sc":
                    _, l, hp, t = step
                    i = SC_ORDER.index((l, hp, t))
                    wait_full(dve, step)
                    link(v.reduce_max(rsum[:, 0:2], T(step)[:].rearrange("p (h m) -> p h m", h=2), axis=AX.X))
                    v.tensor_scalar(mx, rsum, -SCALE, None, ALU.mult).then_inc(S("score_max"), 1)
                    wait_read(dve, step)
                    k = 4 * t + 2 * hp
                    link(v.reciprocal(rsum, sums[:, k:k + 2]))
                    pv = pm[l][2 * hp + t]
                    v.tensor_tensor(pv, pv, each(rsum, MEM), ALU.mult).then_inc(S("p_normed"), 1)
                    dve.wait_ge(S("p_normed"), i + 1)
                elif kind == "mo":
                    _, l, hp = step
                    dve.wait_ge(S("mo_hi"), 2 * l + hp + 1)
                    s = slice(12 + 2 * hp, 14 + 2 * hp)
                    read(step, v.tensor_tensor(oT_lo[l][:, s, :].rearrange("p h t -> p (h t)"), T(step)[:],
                                               oT_hi[l][:, s, :].bitcast(F).rearrange("p h t -> p (h t)"),
                                               ALU.subtract))
                elif kind == "ffnT":
                    _, l, j = step
                    dve.wait_ge(S("uT_hi"), FFN_BLOCKS * l + j + 1)
                    s = slice(2 * j, 2 * j + 2)
                    read(step, v.tensor_tensor(uT_lo[:, s, :].rearrange("p k t -> p (k t)"), T(step)[:],
                                               uT_hi[:, s, :].bitcast(F).rearrange("p k t -> p (k t)"),
                                               ALU.subtract))
                elif kind == "z":
                    h = step[1]
                    l1, ps = abuf[:, h % 2], T(step)[:, 0:384]
                    dve.wait_ge(S("log1p"), h + 1)
                    if h >= 2:
                        wait_full(dve, ("C", h - 2))
                    if h >= 4:
                        wait_full(dve, ("O", h - 4))
                    link(v.scalar_tensor_tensor(lsb[:, h % 4], ps, 0.0, l1, ALU.min, ALU.subtract))
                    read(step, v.scalar_tensor_tensor(spb[:, h % 2], ps, 0.0, l1, ALU.max, ALU.add))
                elif kind == "C":
                    h = step[1]
                    wait_full(dve, step)
                    read(step, v.tensor_tensor(lsb[:, h % 4], lsb[:, h % 4], T(step)[:, 0:384], ALU.subtract))
                elif kind == "O":
                    h = step[1]
                    dve.wait_ge(S("O_hi"), h + 1)
                    read(step, v.tensor_tensor(oT_lo1[:, h, :], T(step)[:, 0:SEQ],
                                               oT_hi1[:, h, :].bitcast(F), ALU.subtract))

            def head_norm(name):
                i = HEAD_NORMS.index(name)
                dve.wait_ge(S("squares"), i + 1)
                link(v.reduce_sum(ssq8, sq[:].rearrange("p (h n) -> p h n", n=P), axis=AX.X))
                rsqrt(r8, ssq8, 8, P, S("head_rstd"), i + 1)
                b = natb(name)[:].rearrange("p t (h n) -> p (t h) n", n=P)
                v.tensor_tensor(b, b, each(r8, P), ALU.mult).then_inc(S("nat_normed"), 1)

            for u in range(-1, UNITS):
                rows = u in ENDS and ENDS[u][0] == "rows"
                if u == -1 or rows:
                    if u == -1:
                        steps(("par", 0))
                    for t in range(TOK):
                        split_to(u + 2 + t)
                        for h in range(2 if rows else 0):
                            wait_acc(dve, u, 2 * t + h)
                            xs_ = xr[:, t, h * COLS:(h + 1) * COLS]
                            v.tensor_tensor(xs_, acc[(ENDS[u][1] + t) % 2][h][:], xs_,
                                            ALU.add).then_inc(S("x_added"), 1)
                        for step in PLAN[u]:
                            if step[0] == "xT" and step[2] == t:
                                steps(step)
                    if u != UNITS - 1:
                        i = ENDS[u][2] + 1 if rows else 0
                        row_norm(i, i + 2 if i else 1)
                    continue
                split_to(u + 3)
                if u in ENDS:
                    kind, a = ENDS[u][:2]
                    name = ENDS[u][2]
                    if kind == "block" and name == "dtq0":
                        dve.wait_ge(S("head_vectors_landed"), 48)
                        for t in range(TOK):
                            wait_acc_read(dve, a, t)
                        b2 = dtv.rearrange("p (t h) -> p t h", t=TOK)
                        v.tensor_tensor(b2, b2, whole(bias_b, TOK), ALU.add).then_inc(S("dt_biased"), 1)
                        dve.wait_ge(S("dt_log"), 2)
                        link(v.scalar_tensor_tensor(dt, dtv, 0.0, dta, ALU.max, ALU.add))
                        v.scalar_tensor_tensor(da.rearrange("p (t h) -> p t h", t=TOK),
                                               dt.rearrange("p (t h) -> p t h", t=TOK), -1.0,
                                               whole(alog_b, TOK), ALU.mult, ALU.mult).then_inc(S("da"), 1)
                    elif kind == "block" and (name in HEAD_NORMS or name == "dtq1"):
                        head_norm("qm0" if name == "dtq1" else name)
                    elif kind == "ffn":
                        l, j = ENDS[u][2:]
                        n = FFN_BLOCKS * l + j
                        if j >= 2:
                            wait_full(dve, ("ffnT", l, j - 2))
                        for t in range(TOK):
                            dve.wait_ge(S("gate_silu"), TOK * n + t + 1)
                            v.scalar_tensor_tensor(un[:, j % 2, t, :], acc[a % 2][t][:, 256:512],
                                                   rstd_x[2 * l + 1][:, t:t + 1], sg[:, j % 2, t, :],
                                                   ALU.mult, ALU.mult).then_inc(acc_free[a % 2], 1)
                for step in PLAN[u]:
                    steps(step)
                if u == 9:
                    row_norm(4, 2)

        @block.tensor
        def _(pe):
            mm = nc.tensor.matmul

            def begin(step):
                i = USES[step]
                if i >= 4:
                    pe.wait_ge(bank_read[i % 4], i // 4)
                return bank[i % 4]

            def tr(dst, src):
                return nc.tensor.transpose(dst, src, ident[:])

            def products(ps, stat_hi, stat_lo, mov_hi, mov_lo, first, last):
                mm(ps, stat_hi, mov_lo, start=first, stop=False)
                mm(ps, stat_hi, mov_hi, start=False, stop=False)
                return mm(ps, stat_lo, mov_hi, start=False, stop=last)

            def wait_acc_free(a, j):
                b = a - 2
                if b < 0:
                    return
                if b in MODE:
                    _, i, t = MODE[b]
                    pe.wait_ge(S("x_added"), 4 * i + 2 * t + j + 1)
                else:
                    wait_acc_read(pe, b, j)

            def col_products(u, a, half, t, width, act_hi, act_lo):
                s = u % RING
                pe.wait_ge(lo_ready, u + 1)
                if half == 0:
                    wait_acc_free(a, t)
                for k in range(UNIT_KT):
                    kt = half * UNIT_KT + k
                    tt, w = slice(t * P, (t + 1) * P), slice(k * width, (k + 1) * width)
                    last = products(acc[a % 2][t][:, 0:width], act_hi[:, kt, tt], act_lo[:, kt, tt],
                                    hi[s][:, w], lo[s][:, w], kt == 0, kt == KT - 1)
                return last

            def row_products(u, a, kt0, t, first, final, act_hi, act_lo):
                s = u % RING
                pe.wait_ge(lo_ready, u + 1)
                for h in range(2):
                    if first:
                        wait_acc_free(a + t, h)
                    for k in range(2):
                        tt, w = slice(t * P, (t + 1) * P), slice(k * D + h * COLS, k * D + (h + 1) * COLS)
                        last = products(acc[(a + t) % 2][h][:], act_hi[:, kt0 + k, tt], act_lo[:, kt0 + k, tt],
                                        hi[s][:, w], lo[s][:, w], first and k == 0, final and k == 1)
                    if final and (t, h) != (1, 1):
                        last.then_inc(acc_done, 1)
                return last

            def steps(step):
                kind = step[0]
                if kind == "gate":
                    return
                b = begin(step)
                if kind == "par" and step[1] == 0:
                    pe.wait_ge(S("gain_landed"), 16)
                    pe.wait_ge(S("masks"), 4)
                    last = nc.tensor.transpose(b[:, 0:16], vrow[0:16, 2, :], ident[0:16, 0:16])
                elif kind == "par":
                    pe.wait_ge(S("vectors_landed"), 144)
                    pe.wait_ge(S("masks"), 4)
                    nc.tensor.transpose(b[:, 0:ROWS_A], vrow[0:ROWS_A, 0, :], ident[0:ROWS_A, 0:ROWS_A])
                    last = nc.tensor.transpose(b[:, P:P + ROWS_B], vrow[0:ROWS_B, 1, :], ident[0:ROWS_B, 0:ROWS_B])
                elif kind == "xT":
                    _, p, t, h = step
                    if p == 0:
                        pe.wait_ge(S(f"x_landed{t}"), 16)
                    else:
                        pe.wait_ge(S("x_added"), 4 * (p - 1) + 2 * t + h + 1)
                    for k in range(4):
                        last = tr(b[:, k * P:(k + 1) * P], xr[:, t, (4 * h + k) * P:(4 * h + k + 1) * P])
                elif kind == "memT":
                    _, t, h = step
                    pe.wait_ge(S("mem_landed"), 32)
                    for k in range(4):
                        last = tr(b[:, k * P:(k + 1) * P], memn[:, t, (4 * h + k) * P:(4 * h + k + 1) * P])
                elif kind == "cs":
                    pe.wait_ge(S("da"), 1)
                    mm(b[:, 0:2 * HEADS], tle[:], da, start=True, stop=True)
                    last = mm(b[:, 2 * HEADS:3 * HEADS], ones[:], da[:, 0:HEADS], start=True, stop=True)
                elif kind == "hT":
                    _, name, h = step
                    pe.wait_ge(S("nat_normed"), HEAD_NORMS.index(name) + 1)
                    for q in range(2):
                        for t in range(TOK):
                            c0 = (2 * h + q) * P
                            last = tr(b[:, q * SEQ + t * P:q * SEQ + (t + 1) * P], natb(name)[:, t, c0:c0 + P])
                elif kind == "xb":
                    _, i, h = step
                    name = ["B", "C", "xs0", "xs1", "xs2"][i]
                    wait_acc_read_all(BLOCK_ACC[name])
                    for q in range(2):
                        for t in range(TOK):
                            c0 = (2 * h + q) * P
                            last = tr(b[:, q * SEQ + t * P:q * SEQ + (t + 1) * P], natb(name)[:, t, c0:c0 + P])
                elif kind == "Bn":
                    pe.wait_ge(S("conv_silu"), 2)
                    for g in range(GROUPS):
                        last = tr(b[:, g * P:(g + 1) * P], bcT[:, g, 0:P])
                elif kind == "xsn":
                    _, j, t = step
                    pe.wait_ge(S("conv_silu"), 2 * (j + 2) + 2)
                    for q in range(4):
                        last = tr(b[:, q * P:(q + 1) * P], xsT[:, q, t * P:(t + 1) * P])
                elif kind == "G":
                    pe.wait_ge(S("conv_silu"), 4)
                    for q in range(2):
                        g = 2 * step[1] + q
                        for c in range(2):
                            o = (2 * q + c) * P
                            last = mm(b[:, o:o + P], bcT[:, g, c * P:(c + 1) * P], bcT[:, 4 + g, c * P:(c + 1) * P],
                                      start=True, stop=True)
                elif kind == "csb":
                    _, g, c, h = step
                    pe.wait_ge(S("da"), 1)
                    for q in range(3):
                        col = c * HEADS + g * HPG + 3 * h + q
                        last = mm(b[:, q * P:(q + 1) * P], da[:, col:col + 1].broadcast_to([P, P]), tle[:],
                                  start=True, stop=True)
                elif kind == "yd":
                    _, g, c = step
                    i = 2 * g + c
                    pe.wait_ge(S("w_scan"), i + 1)
                    pe.wait_ge(S("xpad"), i + 1)
                    for j in range(HPG // 2):
                        for e in range(2):
                            last = mm(b[:, j * P:(j + 1) * P], seg[:, i % 2, 2 * j + e, :], xpad[:, c, 2 * j + e, :],
                                      start=(e == 0), stop=(e == 1))
                elif kind == "st":
                    g = step[1]
                    pe.wait_ge(S("xdte"), g + 1)
                    wait_read(pe, ("Bn",))
                    last = mm(b[:, 0:GW], bn[:, g, :], xdte[:], start=True, stop=True)
                elif kind == "yo":
                    g = step[1]
                    wait_read(pe, ("st", g))
                    last = mm(b[:, 0:GW], bcT[:, 4 + g, P:SEQ], state[:], start=True, stop=True)
                elif kind == "yT":
                    j = step[1]
                    pe.wait_ge(S("y_normed"), TOK * (j // 3 + 1))
                    for q in range(2):
                        for t in range(TOK):
                            c0 = (2 * j + q) * P
                            last = tr(b[:, q * SEQ + t * P:q * SEQ + (t + 1) * P], y[:, t, c0:c0 + P])
                elif kind == "sc":
                    _, l, hp, t = step
                    for h in range(2):
                        wait_read(pe, ("hT", f"km{l}", h))
                        wait_read(pe, ("hT", f"qm{l}", h))
                    for h in range(2):
                        hh = 2 * hp + h
                        last = mm(b[:, h * MEM:(h + 1) * MEM], qmT(l, 2 * hp)[:, h, t * P:(t + 1) * P], kmT[l][:, hh, :],
                                  start=True, stop=True)
                elif kind == "pT":
                    _, l, h = step
                    pe.wait_ge(S("p_normed"), 4 * l + 2 * (h // 2) + 2)
                    for m in range(2):
                        for t in range(TOK):
                            last = tr(b[:, m * SEQ + t * P:m * SEQ + (t + 1) * P],
                                      pm[l][2 * (h // 2) + t][:, h % 2, m * P:(m + 1) * P])
                elif kind == "mo":
                    _, l, hp = step
                    wait_acc_read_all(BLOCK_ACC[f"vm{l}"])
                    for h in range(2):
                        wait_read(pe, ("pT", l, 2 * hp + h))
                    for h in range(2):
                        c0 = (2 * hp + h) * P
                        for m in range(2):
                            last = mm(b[:, h * SEQ:(h + 1) * SEQ], vm[l][:, m, c0:c0 + P], pmT[l][:, h, m, :],
                                      start=(m == 0), stop=(m == 1))
                elif kind == "ffnT":
                    _, l, j = step
                    wait_acc_read_all((A_FFN0, A_FFN1)[l] + j)
                    for q in range(2):
                        for t in range(TOK):
                            last = tr(b[:, q * SEQ + t * P:q * SEQ + (t + 1) * P], un[:, j % 2, t, q * P:(q + 1) * P])
                elif kind == "z":
                    h = step[1]
                    for n in ("k", "q"):
                        wait_read(pe, ("hT", f"{n}{h // 4}", h % 4 // 2))
                    mm(b[:, 0:SEQ], kT[:, h, 0:P], qT[:, h, :], start=True, stop=True)
                    last = mm(b[:, SEQ:SEQ + P], kT[:, h, P:SEQ], qT[:, h, P:SEQ], start=True, stop=True)
                elif kind == "C":
                    h = step[1]
                    sp_ = spb[:, h % 2]
                    pe.wait_ge(S("sp_masked"), h + 1)
                    mm(b[:, 0:SEQ], tgt[:], sp_[:, 0:SEQ], start=True, stop=False)
                    mm(b[:, P:SEQ], ones[:], sp_[:, SEQ:SEQ + P], start=False, stop=True)
                    last = mm(b[:, SEQ:SEQ + P], tgt[:], sp_[:, SEQ:SEQ + P], start=True, stop=True)
                elif kind == "O":
                    h = step[1]
                    w = lsb[:, h % 4]
                    pe.wait_ge(S("w_masked"), h + 1)
                    if h % 4 == 0:
                        wait_acc_read_all(BLOCK_ACC[f"v{h // 4}"])
                    mm(b[:, 0:SEQ], vn[:, 0, h * P:(h + 1) * P], w[:, 0:SEQ], start=True, stop=False)
                    last = mm(b[:, P:SEQ], vn[:, 1, h * P:(h + 1) * P], w[:, SEQ:SEQ + P], start=False, stop=True)
                filled(step, last)

            def wait_acc_read_all(a):
                for t in range(TOK):
                    wait_acc_read(pe, a, t)

            def inputs_ready(p, t):
                for h in range(2):
                    wait_read(pe, ("memT", t, h) if p == 4 else ("xT", p, t, h))

            def column_phase(u0, a0, p, widths, memory=()):
                for i, width in enumerate(widths):
                    u, a = u0 + 2 * i, a0 + i
                    operand = (mT_hi, mT_lo) if i in memory else (aT_hi, aT_lo)
                    if i == 0:
                        inputs_ready(p, 0)
                        col_products(u, a, 0, 0, width, *operand)
                        for h in range(2):
                            steps(("xT", p, 1, h))
                        col_products(u + 1, a, 1, 0, width, *operand).then_inc(acc_done, 1)
                        inputs_ready(p, 1)
                        col_products(u, a, 0, 1, width, *operand).then_inc(unit_used, 1)
                        for step in PLAN[u]:
                            steps(step)
                        col_products(u + 1, a, 1, 1, width, *operand).then_inc(unit_used, 1)
                        for step in PLAN[u + 1]:
                            steps(step)
                        continue
                    if memory and i == min(memory):
                        for t in range(TOK):
                            inputs_ready(4, t)
                    for half in range(2):
                        last = col_products(u + half, a, half, 0, width, *operand)
                        if half == 1:
                            last.then_inc(acc_done, 1)
                        col_products(u + half, a, half, 1, width, *operand).then_inc(unit_used, 1)
                        for step in PLAN[u + half]:
                            steps(step)

            def row_phase(u0, a0, p, rows, needs, act_hi, act_lo):
                def part(i, t):
                    return row_products(u0 + i, a0, rows[i], t, i == 0, i == len(rows) - 1, act_hi, act_lo)

                n = len(rows)
                for i in range(n - 2):
                    for step in needs(rows[i]):
                        wait_read(pe, step)
                    part(i, 0)
                    part(i, 1).then_inc(unit_used, 1)
                    for step in PLAN[u0 + i]:
                        steps(step)
                for i in (n - 2, n - 1):
                    for step in needs(rows[i]):
                        wait_read(pe, step)
                    part(i, 0)
                part(n - 2, 1).then_inc(unit_used, 1)
                for h in range(2 if p else 0):
                    steps(("xT", p, 0, h))
                part(n - 1, 1).then_inc(unit_used, 1)

            for step in PLAN[-1]:
                if step[:1] + step[2:3] != ("xT", 1):
                    steps(step)
            column_phase(U_IN0, A_IN0, 0, [b[2] for b in IN0], [i for i, b in enumerate(IN0) if b[0][1:2] == "m"])
            row_phase(U_OUT0, A_OUT0, 1, OUT0_ROWS,
                      lambda kt: [("mo", 0, (kt - 12) // 2)] if kt >= 12 else [("yT", kt // 2)], oT_hi0, oT_lo0)
            column_phase(U_FFN0, A_FFN0, 1, [COLS] * FFN_BLOCKS)
            row_phase(U_DOWN0, A_DOWN0, 2, DOWN_ROWS, lambda kt: [("ffnT", 0, kt // 2)], uT_hi, uT_lo)
            column_phase(U_IN1, A_IN1, 2, [b[2] for b in IN1])
            row_phase(U_OUT1, A_OUT1, 3, OUT1_ROWS,
                      lambda kt: [("mo", 1, (kt - 12) // 2)] if kt >= 12 else [("O", kt), ("O", kt + 1)],
                      oT_hi1, oT_lo1)
            column_phase(U_FFN1, A_FFN1, 3, [COLS] * FFN_BLOCKS)
            row_phase(U_DOWN1, A_DOWN1, None, DOWN_ROWS, lambda kt: [("ffnT", 1, kt // 2)], uT_hi, uT_lo)


_INS = ["x", "mem", "mix_norm_g", "ffn_norm_g", "mem_norm_g", "mem_w_kv", "mem_q_norm_g", "mem_k_norm_g",
        "ssd_w_in", "ssd_conv_w", "ssd_conv_b", "ssd_dt_bias", "ssd_a_log", "ssd_d", "ssd_norm_g", "ssd_w_out",
        "sb_w_in", "sb_q_norm_g", "sb_k_norm_g", "sb_w_out", "ffn_w_gate_up", "ffn_w_down"]


def kernel(**inputs):
    import numpy as np
    import concourse.bacc as bacc
    from concourse.bass_utils import run_bass_kernel_spmd

    nc = bacc.Bacc("TRN2", target_bir_lowering=False, num_devices=1)
    arrays, args = {}, []
    for name in _INS:
        a = np.ascontiguousarray(inputs[name])
        arrays[f"in_{name}"] = a
        args.append(nc.dram_tensor(f"in_{name}", a.shape, mybir.dt.from_np(a.dtype), kind="ExternalInput").ap())
    out = nc.dram_tensor("out", (1, SEQ, D), mybir.dt.float32, kind="ExternalOutput").ap()
    trunk(nc, *args, out)
    return run_bass_kernel_spmd(nc, [arrays], core_ids=[0]).results[0]["out"]
```

```python
from contextlib import ExitStack

import concourse.bass as bass
from concourse import mybir

P = 128
SEQ, D, MEM = 256, 1024, 256
TOK = SEQ // P
KT = D // P
MIX = 2 * D
MEM_W = MIX // 4
MEM_HEADS = 4
INNER = MIX - MEM_W
GROUPS, STATE, HP = 4, 128, 64
HEADS = INNER // HP
HPG = HEADS // GROUPS
GW = INNER // GROUPS
CONV = 4
CONV_DIM = INNER + 2 * GROUPS * STATE
SB_HEADS = INNER // P
FFN = ((-(-8 * D // 3) + 255) // 256) * 256
EPS = 1e-6
FT = CONV_DIM // P
MT = MIX // P
HT = FFN // P
SCALE = float(P) ** -0.5

RING = 4
COLS = 512
UNIT_KT = 4

QM0 = INNER + CONV_DIM
DTQ = (HEADS + MEM_W) // 2
XB = INNER
IN0 = [("dtq0", QM0, DTQ), ("dtq1", QM0 + DTQ, DTQ),
       ("B", XB + INNER, COLS), ("C", XB + INNER + COLS, COLS),
       ("xs0", XB, COLS), ("xs1", XB + COLS, COLS), ("xs2", XB + 2 * COLS, COLS),
       ("km0", 0, COLS), ("vm0", MEM_W, COLS), ("km1", 0, COLS), ("vm1", MEM_W, COLS),
       ("z0", 0, COLS), ("z1", COLS, COLS), ("z2", 2 * COLS, COLS)]
IN1 = [("qm1", 3 * INNER, COLS)] + [(f"k{j}", INNER + j * COLS, COLS) for j in range(3)] + \
      [b for j in range(3) for b in ((f"q{j}", j * COLS, COLS), (f"v{j}", 2 * INNER + j * COLS, COLS))]
FFN_BLOCKS = FFN // 256
OUT0_ROWS = [12, 14, 0, 2, 4, 6, 8, 10]
OUT1_ROWS = [0, 2, 4, 6, 8, 10, 12, 14]
DOWN_ROWS = list(range(0, HT, 2))

U_IN0 = 0
U_OUT0 = U_IN0 + 2 * len(IN0)
U_FFN0 = U_OUT0 + len(OUT0_ROWS)
U_DOWN0 = U_FFN0 + 2 * FFN_BLOCKS
U_IN1 = U_DOWN0 + len(DOWN_ROWS)
U_OUT1 = U_IN1 + 2 * len(IN1)
U_FFN1 = U_OUT1 + len(OUT1_ROWS)
U_DOWN1 = U_FFN1 + 2 * FFN_BLOCKS
UNITS = U_DOWN1 + len(DOWN_ROWS)
U_SEG = 17

A_IN0 = 0
A_OUT0 = A_IN0 + len(IN0)
A_FFN0 = A_OUT0 + 2
A_DOWN0 = A_FFN0 + FFN_BLOCKS
A_IN1 = A_DOWN0 + 2
A_OUT1 = A_IN1 + len(IN1)
A_FFN1 = A_OUT1 + 2
A_DOWN1 = A_FFN1 + FFN_BLOCKS

GC = [(g, c) for g in range(GROUPS) for c in range(TOK)]

PLAN = {u: [] for u in range(-1, UNITS)}


def _plan():
    def at(u, *steps):
        PLAN[u] += steps

    def block_end(name):
        names = [n for n, _, _ in IN0]
        if name in names:
            return U_IN0 + 2 * names.index(name) + 1
        return U_IN1 + 2 * [n for n, _, _ in IN1].index(name) + 1

    def input_transposes(u, p):
        at(u, *[("xT", p, t, h) for t in range(TOK) for h in range(2)])

    at(-1, ("par", 0))
    input_transposes(-1, 0)
    at(1, ("par", 1))
    at(2, ("dt",))
    at(3, ("cs",))
    at(8, ("csT",))
    at(5, ("hT", "qm0", 0), ("hT", "qm0", 1))
    for i, u in enumerate((6, 8, 10, 12, 14)):
        for h in range(2):
            at(u + h, ("xb", i, h))
            if i >= 3:
                continue
            at(u + h + 1, ("silu", i, h))
        if i == 0:
            at(7, ("memT", 0, 0), ("memT", 0, 1))
        elif i == 1:
            at(9, ("memT", 1, 0), ("memT", 1, 1))
        elif i == 2:
            at(11, ("Bn",))
        elif i == 3:
            at(12, ("G", 0), ("G", 1))
        if i >= 3:
            at(u + 1, ("xsn", i - 3, 0), ("xsn", i - 3, 1), ("silu", i, 0))
            if i == 3:
                at(u + 2, ("silu", i, 1))
    at(16, ("silu", 4, 1))
    at(17, ("xsn", 2, 0), ("xsn", 2, 1))
    at(17, ("hT", "km0", 0), ("hT", "km0", 1))
    for i in range(len(GC) + 2):
        if 1 <= i <= len(GC):
            at(U_SEG + i, ("seg", *GC[i - 1]), ("segm", *GC[i - 1]))
        if i >= 2:
            g, c = GC[i - 2]
            at(U_SEG + i, ("yd", g, c))
            at(U_SEG + i, ("yo", g) if c else ("st", g))

    def memory_attention(l, u_scores, u_p, u_o):
        for u, (hp, t) in zip(u_scores, [(0, 0), (0, 1), (1, 0), (1, 1)]):
            at(u, ("sc", l, hp, t))
            at(u + 1, ("pn", l, hp, t))
        for hp in range(2):
            at(u_p[2 * hp], ("pT", l, 2 * hp))
            at(u_p[2 * hp + 1], ("pT", l, 2 * hp + 1))
            at(u_o[hp], ("mo", l, hp))

    memory_attention(0, (21, 22, 23, 24), (23, 24, 26, 26), (26, 27))
    at(25, ("gate", 0))
    at(27, ("yT", 0), ("yT", 1), ("gate", 1))
    at(28, ("yT", 2))
    at(29, ("hT", "km1", 0), ("hT", "km1", 1))
    at(31, *[("yT", j) for j in range(3, 6)])
    input_transposes(U_FFN0 - 1, 1)
    for l, u in ((0, U_FFN0), (1, U_FFN1)):
        for j in range(FFN_BLOCKS):
            at(u + 2 * j + 2, ("ffnT", l, j))
    input_transposes(U_IN1 - 1, 2)
    for n in ("qm1", "k0", "k1", "k2", "q0", "q1", "q2"):
        at(block_end(n) + 2, ("hT", n, 0), ("hT", n, 1))
    u = block_end("v0") + 1
    late = []
    for p in range(SB_HEADS // 2):
        a, b = 2 * p, 2 * p + 1
        at(u, ("z", a), ("z", b))
        at(u + 1, ("C", a), ("C", b))
        late += [(u + 2, ("O", a), ("O", b))]
        u += 2
    for step in late:
        at(*step)
    e = block_end("q2")
    memory_attention(1, (e, e, e + 2, e + 2), (e + 4, e + 4, e + 7, e + 7), (e + 6, e + 8))
    input_transposes(U_FFN1 - 1, 3)


_plan()

NO_BANK = ("gate", "silu", "seg", "segm", "pn", "dt")
EARLY, MIDDLE = ("seg", "pn"), ("segm",)
USES = {s: i for i, s in enumerate(s for u in sorted(PLAN) for s in PLAN[u] if s[0] not in NO_BANK)}
NAT = {"qm0": ("hT", "qm0", 1), "B": ("xb", 0, 1), "C": ("xb", 1, 1), "xs0": ("xb", 2, 1),
       "xs1": ("xb", 3, 1), "xs2": ("xb", 4, 1), "km0": ("hT", "km0", 1), "km1": ("hT", "km1", 1)}
NAT.update({n: ("hT", n, 1) for n in ("qm1", "k0", "k1", "k2", "q0", "q1", "q2")})
NAT_ORDER = list(NAT)
HEAD_NORMS = [n for n in NAT_ORDER if n[0] in "kq"]
CONV_TILES = [12, 16, 0, 4, 8]


def trunk(nc, x, mem, mix_norm_g, ffn_norm_g, mem_norm_g, mem_w_kv, mem_q_norm_g, mem_k_norm_g,
          ssd_w_in, ssd_conv_w, ssd_conv_b, ssd_dt_bias, ssd_a_log, ssd_d, ssd_norm_g, ssd_w_out,
          sb_w_in, sb_q_norm_g, sb_k_norm_g, sb_w_out, ffn_w_gate_up, ffn_w_down, out):
    F, R, I32 = mybir.dt.float32, mybir.dt.float32r, mybir.dt.int32
    ACT, ALU, AX = mybir.ActivationFunctionType, mybir.AluOpType, mybir.AxisListType

    ctx = ExitStack()
    with ctx:
        def sb(name, shape, dt=F):
            return ctx.enter_context(nc.sbuf_tensor(name, shape, dt))

        def under(specs):
            guards = [nc.sbuf_tensor(*s) for s in specs]
            made = [g.__enter__() for g in guards]
            for g in reversed(guards):
                g.__exit__(None, None, None)
            return made

        UW = UNIT_KT * COLS
        raw = under([(f"raw{i}", [P, UW], F) for i in range(RING)])
        lo = [sb(f"lo{i}", [P, UW], R) for i in range(RING)]
        hi = [sb(f"hi{i}", [P, UW], R) for i in range(RING)]
        aT_hi = sb("aT_hi", [P, KT, SEQ], R)
        aT_lo = sb("aT_lo", [P, KT, SEQ], R)
        xr = sb("xr", [P, TOK, D])
        nat = [sb(f"nat{i}", [P, TOK, COLS]) for i in range(2)]
        sq = sb("sq", [P, D])
        hg2 = sb("hg", [P, 2, 4, P])
        hg = [hg2[:, i] for i in range(2)]
        ident = sb("ident", [P, P])
        tle = sb("tle", [P, P])
        tlt = sb("tlt", [P, P])
        tgt = sb("tgt", [P, P])
        ones = sb("ones", [P, P])
        ROWS_A, ROWS_B = 80 + 20 + 8, 16 + 12 + 6
        vrow = sb("vrow", [P, 3, P])
        vcol = sb("vcol", [P, ROWS_A + ROWS_B + 16])
        kmT = [sb(f"kmT{l}", [P, MEM_HEADS, MEM]) for l in range(2)]
        vm = [sb(f"vm{l}", [P, 2, MEM_W]) for l in range(2)]
        small = sb("small", [P, 480])
        taken = [0]

        def cols(n):
            taken[0] += n
            return small[:, taken[0] - n:taken[0]]

        bias_b, alog_b, d_b = cols(HEADS), cols(HEADS), cols(HEADS)
        dtv, dta, dt = cols(2 * HEADS), cols(2 * HEADS), cols(2 * HEADS)
        da, cs, ecs, dte = cols(2 * HEADS), cols(2 * HEADS), cols(HEADS), cols(HEADS)
        ssq_x, rstd_x = cols(2), [cols(2) for _ in range(5)]
        ssq8, r8, v8, h8, t8 = cols(8), cols(8), cols(8), cols(8), cols(8)
        ssqy, ry = cols(8), cols(8)
        mx, sums, rsum = cols(4), cols(8), cols(2)
        gq_scaled = cols(1)

        oT_hi1, oT_lo1, qT, kT, vn, abuf, lsb, spb = under(
            [("oT_hi1", [P, MT, SEQ], R), ("oT_lo1", [P, MT, SEQ], R),
             ("qT", [P, SB_HEADS, SEQ], F), ("kT", [P, SB_HEADS, SEQ], F),
             ("vn", [P, 2, INNER], F), ("abuf", [P, 2, 384], F), ("lsb", [P, 4, 384], F),
             ("spb", [P, 2, 384], F)])
        uT_hi, uT_lo, sg, un = under(
            [("uT_hi", [P, HT, SEQ], R), ("uT_lo", [P, HT, SEQ], R),
             ("sg", [P, 2, TOK, 256], F), ("un", [P, 2, TOK, 256], F)])
        bcT, xsT, bn, gm, xpad, xdte, seg = under(
            [("bcT", [P, 8, SEQ], F), ("xsT", [P, 4, SEQ], F), ("bn", [P, 4, P], F),
             ("gm", [P, GROUPS, 2, P], F), ("xpad", [P, 2, HPG, P], F), ("xdte", [P, GW], F),
             ("seg", [P, 2, HPG, P], F)])
        oT_hi0 = sb("oT_hi0", [P, MT, SEQ], R)
        oT_lo0 = sb("oT_lo0", [P, MT, SEQ], R)
        y = sb("y", [P, TOK, INNER])
        zs = sb("zs", [P, TOK, INNER])
        conv = [zs[:, i, D:D + 512].rearrange("p (q t) -> p q t", q=2) for i in range(2)]
        p0, pT0 = under([("p0", [P, 2 * TOK, 2, MEM], F), ("pT0", [P, 2, 2, SEQ], F)])
        mT_hi = sb("mT_hi", [P, KT, SEQ], R)
        mT_lo = sb("mT_lo", [P, KT, SEQ], R)
        qmT0 = sb("qmT0", [P, MEM_HEADS, SEQ])
        state = sb("state", [P, GW])
        yoff = sb("yoff", [P, GW])
        segs = [seg[:, 0], seg[:, 1], hg2[:].rearrange("p a k t -> p (a k) t")[:, 0:HPG, :]]
        memn = zs[:, :, 0:D]
        oT_hi, oT_lo = (oT_hi0, oT_hi1), (oT_lo0, oT_lo1)
        pm = ([p0[:, i] for i in range(4)],
              [b.rearrange("p a (b m) -> p (a b) m", m=MEM)[:, 2 * i:2 * i + 2, :] for b in (kmT[0][:], vm[0][:])
               for i in range(2)])
        pmT = (pT0[:], sq[:].rearrange("p (h m t) -> p h m t", h=2, m=2))

        def qmT(l, h):
            return qmT0[:, h:h + 2, :] if l == 0 else hg[h // 2].rearrange("p (a b) t -> p a (b t)", a=2)

        acc = [[ctx.enter_context(nc.psum_tensor(f"acc{i}{j}", [P, COLS], F)) for j in range(2)]
               for i in range(2)]
        bank = [ctx.enter_context(nc.psum_tensor(f"bank{i}", [P, COLS], F)) for i in range(4)]

        cs_rows = nc.dram_tensor("cs_rows", (TOK * GROUPS, HPG * P), F, kind="Internal").ap()

        sems = {}

        def S(name):
            if name not in sems:
                sems[name] = ctx.enter_context(nc.semaphore(name))
            return sems[name]

        raw_landed = [S(f"raw_landed{i}") for i in range(RING)]
        hi_ready, lo_ready, unit_used = S("hi_ready"), S("lo_ready"), S("unit_used")
        acc_done = S("acc_done")
        acc_free = [S(f"acc_free{i}") for i in range(2)]
        bank_full = [S(f"bank_full{i}") for i in range(4)]
        bank_read = [S(f"bank_read{i}") for i in range(4)]

        def col_unit(w, c0, width, half):
            rows = w[half * UNIT_KT * P:(half + 1) * UNIT_KT * P, c0:c0 + width]
            return rows.rearrange("(t p) n -> p t n", p=P)

        def gate_up_unit(l, j, half):
            return [col_unit(ffn_w_gate_up[l], g * FFN + j * 256, 256, half) for g in range(2)]

        def row_unit(w, kt):
            return w[kt * P:(kt + 2) * P, :].rearrange("(t p) n -> p t n", p=P)

        SRC = []
        for name, c0, width in IN0:
            w = mem_w_kv[int(name[2])] if name[1:2] == "m" else ssd_w_in[0]
            SRC += [(col_unit(w, c0, width, h), UNIT_KT * width) for h in range(2)]
        SRC += [(row_unit(ssd_w_out[0], kt), UW) for kt in OUT0_ROWS]
        SRC += [(gate_up_unit(0, j, h), UW) for j in range(FFN_BLOCKS) for h in range(2)]
        SRC += [(row_unit(ffn_w_down[0], kt), UW) for kt in DOWN_ROWS]
        SRC += [(col_unit(sb_w_in[0], c0, w_, h), UNIT_KT * w_) for _, c0, w_ in IN1 for h in range(2)]
        SRC += [(row_unit(sb_w_out[0], kt), UW) for kt in OUT1_ROWS]
        SRC += [(gate_up_unit(1, j, h), UW) for j in range(FFN_BLOCKS) for h in range(2)]
        SRC += [(row_unit(ffn_w_down[1], kt), UW) for kt in DOWN_ROWS]

        LANDED = []
        for u, (src, _) in enumerate(SRC):
            LANDED.append((LANDED[u - RING] if u >= RING else 0) + 16 * (2 if isinstance(src, list) else 1))

        ENDS = {}
        for i, (name, _, width) in enumerate(IN0):
            ENDS[U_IN0 + 2 * i + 1] = ("block", A_IN0 + i, name, width)
        for i, (name, _, width) in enumerate(IN1):
            ENDS[U_IN1 + 2 * i + 1] = ("block", A_IN1 + i, name, width)
        for l, (u, a) in enumerate(((U_FFN0, A_FFN0), (U_FFN1, A_FFN1))):
            for j in range(FFN_BLOCKS):
                ENDS[u + 2 * j + 1] = ("ffn", a + j, l, j)
        for i, (u, a) in enumerate(((U_FFN0, A_OUT0), (U_IN1, A_DOWN0), (U_FFN1, A_OUT1), (UNITS, A_DOWN1))):
            ENDS[u - 1] = ("rows", a, i)

        done_before, total = {}, 0
        for u in sorted(ENDS):
            kind, a = ENDS[u][:2]
            done_before[a] = total
            total += 3 if kind == "rows" else 1

        def wait_acc(eng, u, j, rows_j=None):
            kind, a = ENDS[u][:2]
            if j == (3 if kind == "rows" else 1):
                eng.wait_ge(unit_used, u + 1)
            else:
                eng.wait_ge(acc_done, done_before[a] + j + 1)

        ROWS_AT = [A_OUT0, A_DOWN0, A_OUT1, A_DOWN1]
        MODE = {}
        for i, a0 in enumerate(ROWS_AT):
            for t in range(TOK):
                MODE[a0 + t] = ("rows", i, t)
        col_free = {}
        n_col = [0, 0]
        for a in range(A_DOWN1 + 2):
            if a not in MODE:
                n_col[a % 2] += TOK
            col_free[a] = n_col[a % 2]

        def wait_acc_read(eng, a, j):
            eng.wait_ge(acc_free[a % 2], col_free[a] - TOK + j + 1)

        def T(step):
            return bank[USES[step] % 4]

        def wait_full(eng, step):
            eng.wait_ge(bank_full[USES[step] % 4], USES[step] // 4 + 1)

        def wait_read(eng, step):
            eng.wait_ge(bank_read[USES[step] % 4], USES[step] // 4 + 1)

        def filled(step, ins):
            ins.then_inc(bank_full[USES[step] % 4], 1)

        def read(step, ins):
            ins.then_inc(bank_read[USES[step] % 4], 1)

        BLOCK_ACC = {n: A_IN0 + i for i, (n, _, _) in enumerate(IN0)}
        BLOCK_ACC.update({n: A_IN1 + i for i, (n, _, _) in enumerate(IN1)})

        def natb(name):
            return nat[NAT_ORDER.index(name) % 2]

        def each(ap, n):
            return ap.unsqueeze(2).broadcast_to([P, ap.shape[1], n])

        def whole(ap, k):
            return ap.unsqueeze(1).broadcast_to([P, k, ap.shape[1]])

        def heads_of(c, g, n=HPG, first=0):
            at = c * HEADS + g * HPG + first
            return slice(at, at + n)

        def conv_w(j, ft):
            return vcol[:, j * FT + ft:j * FT + ft + 1]

        def conv_b(ft):
            return vcol[:, 80 + ft:81 + ft]

        MIX_G = ROWS_A + ROWS_B
        XT_GAIN = [MIX_G, ROWS_A, MIX_G + KT, ROWS_A + KT, 100]
        NORM_G = ROWS_A + 16
        MQ, MK, SQ_, SK_ = ROWS_A + 28, ROWS_A + 30, ROWS_A + 32, ROWS_A + 33

        def xt_index(step):
            if step[0] == "memT":
                return 4 + 2 * step[1] + step[2]
            _, p, t, h = step
            return (0 if p == 0 else 4 + 4 * p) + 2 * t + h

        SC_ORDER = [(l, hp, t) for l in range(2) for hp in range(2) for t in range(TOK)]

        block = ctx.enter_context(nc.Block())

        @block.sync
        def _(sp):
            def x_in(t):
                for h in range(2):
                    c = slice(h * COLS, (h + 1) * COLS)
                    sp.dma_start(xr[:, t, c], x[0, t * P:(t + 1) * P, c]).then_inc(S(f"x_landed{t}{h}"), 16)

            def cs_out():
                wait_read(sp, ("csT",))
                sp.dma_start(cs_rows.rearrange("k (h t) -> (k h) t", h=HPG),
                             vrow[0:TOK * HEADS, 2, :]).then_inc(S("cs_rows_written"), 16)

            def decays_in(i):
                g, c = GC[i]
                sp.wait_ge(S("cs_rows_written"), 16)
                if i >= 3:
                    wait_full(sp, ("yd", *GC[i - 3]))
                k = c * GROUPS + g
                sp.dma_start(segs[i % 3].rearrange("p h t -> p (h t)"),
                             cs_rows[k:k + 1, :].broadcast_to([P, HPG * P])).then_inc(S(f"decays_landed{i % 3}"), 16)

            for u in range(UNITS):
                if u in (0, 2):
                    x_in(u // 2)
                if u == RING + 1:
                    for t in range(TOK):
                        sp.dma_start(memn[:, t, :], mem[0, t * P:(t + 1) * P, :]).then_inc(S("mem_landed"), 16)
                src, n = SRC[u]
                if u >= RING:
                    sp.wait_ge(unit_used, u - RING + 1)
                srcs = src if isinstance(src, list) else [src]
                dst = raw[u % RING][:, 0:n].rearrange("p (t g n) -> p t g n", t=srcs[0].shape[1], g=len(srcs))
                for g, part in enumerate(srcs):
                    sp.dma_start(dst[:, :, g, :], part).then_inc(raw_landed[u % RING], 16)
                if u == 8 + RING:
                    cs_out()
                if U_SEG - 1 <= u - RING < U_SEG - 1 + len(GC):
                    decays_in(u - RING - U_SEG + 1)

        @block.gpsimd
        def _(pool):
            nc.gpsimd.memset(ones[:], 1.0).then_inc(S("ones_made"), 1)
            pool.wait_ge(S("ones_made"), 1)
            for m, op, cm, step in ((ident, ALU.is_equal, 1, -1), (tle, ALU.is_ge, -1, 1),
                                    (tlt, ALU.is_gt, -1, 1), (tgt, ALU.is_gt, 1, -1)):
                nc.gpsimd.affine_select(out=m[:], in_=ones[:], compare_op=op, fill=0.0, base=0,
                                        pattern=[[step, P]], channel_multiplier=cm).then_inc(S("masks"), 1)
            rows = [(0, 0, ssd_conv_w[0].rearrange("j (f p) -> (j f) p", p=P)),
                    (0, 80, ssd_conv_b[0].rearrange("(f p) -> f p", p=P)),
                    (0, 100, mem_norm_g.rearrange("(f p) -> f p", p=P)),
                    (1, 0, ffn_norm_g.rearrange("l (f p) -> (l f) p", p=P)),
                    (1, 16, ssd_norm_g[0].rearrange("(f p) -> f p", p=P)),
                    (1, 28, mem_q_norm_g), (1, 30, mem_k_norm_g), (1, 32, sb_q_norm_g), (1, 33, sb_k_norm_g)]
            for b, r, v in rows:
                pool.dma_start(vrow[r:r + v.shape[0], b, :], v).then_inc(S("vectors_landed"), 16)
            for dst, v in ((bias_b, ssd_dt_bias), (alog_b, ssd_a_log), (d_b, ssd_d)):
                pool.dma_start(dst, v.broadcast_to([P, HEADS])).then_inc(S("head_vectors_landed"), 16)
            nc.gpsimd.memset(xpad[:].rearrange("p c h n -> p (c h n)"), 0.0).then_inc(S("xpad_clear"), 1)
            pool.wait_ge(S("xpad_clear"), 1)

            def scan_inputs(g, c):
                if g == 0 and c == 0:
                    for j in range(3):
                        for t in range(TOK):
                            wait_read(pool, ("xsn", j, t))
                    pool.wait_ge(S("dtdte"), 1)
                if g:
                    wait_full(pool, ("yd", g - 1, c))
                xg = y[:, c, g * GW:(g + 1) * GW].rearrange("p (j e n) -> p j e n", e=2, n=HP)
                xp = xpad[:, c].rearrange("p (j e) n -> p j e n", e=2)
                dg = dt[:, heads_of(c, g)].rearrange("p (j e) -> p j e", e=2)
                for e in range(2):
                    last = nc.gpsimd.tensor_tensor(xp[:, :, e, e * HP:(e + 1) * HP], xg[:, :, e, :],
                                                   each(dg[:, :, e], HP), ALU.mult)
                last.then_inc(S("xpad"), 1)
                if c == 0:
                    if g:
                        wait_full(pool, ("st", g - 1))
                    nc.gpsimd.tensor_tensor(xdte[:].rearrange("p (h n) -> p h n", n=HP),
                                            y[:, 0, g * GW:(g + 1) * GW].rearrange("p (h n) -> p h n", n=HP),
                                            each(dte[:, heads_of(0, g)], HP), ALU.mult).then_inc(S("xdte"), 1)
                pool.wait_ge(S("xpad"), 2 * g + c + 1)
                pool.wait_ge(S("xdte"), g + 1)
                yg = y[:, c, g * GW:(g + 1) * GW].rearrange("p (h n) -> p h n", n=HP)
                nc.gpsimd.tensor_tensor(yg, yg, each(d_b[:, heads_of(0, g)], HP), ALU.mult).then_inc(S("skip"), 1)

            def diag_mask(buf, s):
                v = buf[:, s].rearrange("p (b t) -> p b t", t=P)[:, 0:3:2, :]
                return nc.gpsimd.tensor_tensor(v, v, whole(tlt[:], 2), ALU.mult)

            for u in range(-1, UNITS):
                for step in PLAN[u]:
                    kind = step[0]
                    if kind == "seg":
                        scan_inputs(step[1], step[2])
                    elif kind == "yo":
                        g = step[1]
                        wait_read(pool, ("yd", g, 1))
                        wait_read(pool, step)
                        yg = y[:, 1, g * GW:(g + 1) * GW]
                        nc.gpsimd.tensor_tensor(yg, yg, yoff[:], ALU.add).then_inc(S("y_whole"), 1)
                    elif kind == "z":
                        wait_read(pool, step)
                        diag_mask(spb, step[1] % 2).then_inc(S("sp_masked"), 1)
                    elif kind == "C":
                        pool.wait_ge(S("w_exp"), step[1] + 1)
                        diag_mask(lsb, step[1] % 4).then_inc(S("w_masked"), 1)

        @block.scalar
        def _(act):
            made = [0]

            def link(ins):
                made[0] += 1
                ins.then_inc(S("act_seq"), 1)
                act.wait_ge(S("act_seq"), made[0])

            def f(out_, in_, func=ACT.Copy, **k):
                return nc.scalar.activation(out_, in_, func, **k)

            act.dma_start(vrow[0:16, 2, :], mix_norm_g.rearrange("l (f p) -> (l f) p", p=P)).then_inc(S("gain_landed"), 16)
            act.preload_act_table_set("natural_log_exp_and_others")
            split_at = [0]

            def split_to(u):
                while split_at[0] < min(u, UNITS):
                    v = split_at[0]
                    n = SRC[v][1]
                    act.wait_ge(raw_landed[v % RING], LANDED[v])
                    f(hi[v % RING][:, 0:n], raw[v % RING][:, 0:n]).then_inc(hi_ready, 1)
                    split_at[0] += 1

            ssq_sums = [0]

            def sum_squares(p, src):
                i = ssq_sums[0]
                for t in range(TOK):
                    f(sq[:], src[:, t, :], ACT.Square, accum_out=ssq_x[:, t:t + 1]).then_inc(S("x_ssq"), 1)
                    act.wait_ge(S("x_ssq"), TOK * i + t + 1)
                ssq_sums[0] += 1

            def end_block(u, a, name, width):
                rs = rstd_x[4 if name[1:2] == "m" and name[0] in "kv" else (0 if u < U_OUT0 else 2)]
                if name == "dtq0":
                    act.wait_ge(S("rstd"), 1)
                if name == "km0":
                    act.wait_ge(S("rstd"), 2)
                if name == "qm1":
                    act.wait_ge(S("rstd"), 4)
                if name in NAT_ORDER and NAT_ORDER.index(name) >= 2:
                    wait_full(act, NAT[NAT_ORDER[NAT_ORDER.index(name) - 2]])
                for t in range(TOK):
                    wait_acc(act, u, t)
                    ps, r = acc[a % 2][t], rs[:, t:t + 1]
                    if name == "dtq0":
                        link(f(dtv[:, t * HEADS:(t + 1) * HEADS], ps[:, 0:HEADS], scale=r))
                        last = f(natb("qm0")[:, t, 0:width - HEADS], ps[:, HEADS:width], scale=r)
                    elif name == "dtq1":
                        last = f(natb("qm0")[:, t, DTQ - HEADS:MEM_W], ps[:, 0:width], scale=r)
                    elif name[0] == "z":
                        j = int(name[1])
                        last = f(zs[:, t, j * COLS:(j + 1) * COLS], ps[:], ACT.Silu if j else ACT.Copy, scale=r)
                    elif name[:2] == "vm":
                        last = f(vm[int(name[2])][:, t, :], ps[:], scale=r)
                    elif name[0] == "v":
                        j = int(name[1])
                        last = f(vn[:, t, j * COLS:(j + 1) * COLS], ps[:], scale=r)
                    else:
                        last = f(natb(name)[:, t, :], ps[:], scale=r)
                    last.then_inc(acc_free[a % 2], 1)
                name = "qm0" if name == "dtq1" else name
                if name in HEAD_NORMS:
                    i = HEAD_NORMS.index(name)
                    wait_acc_read(act, a, 1)
                    wait_acc_read(act, a - 1, 1)
                    if i:
                        act.wait_ge(S("nat_normed"), i)
                    f(sq[:], natb(name)[:].rearrange("p t n -> p (t n)"), ACT.Square).then_inc(S("squares"), 1)

            def dt_scan():
                act.wait_ge(S("dt_biased"), 1)
                link(f(dta, dtv, ACT.Abs))
                link(f(dta, dta, ACT.Exp, scale=-1.0))
                f(dta, dta, ACT.Ln, bias=1.0).then_inc(S("dt_log"), 1)
                act.wait_ge(S("head_vectors_landed"), 48)
                f(alog_b, alog_b, ACT.Exp).then_inc(S("dt_log"), 1)

            def step_xT(step):
                i = xt_index(step)
                mem_ = step[0] == "memT"
                t, h = step[-2:]
                dst = (mT_hi if mem_ else aT_hi)[:, 4 * h:4 * h + 4, t * P:(t + 1) * P]
                act.wait_ge(S("hg"), i + 1)
                f(dst, hg[i % 2]).then_inc(S("aT_hi"), 1)

            def conv_first(i, h):
                step, n = ("xb", i, h), 2 * i + h
                ft = CONV_TILES[i] + 2 * h
                wait_full(act, step)
                if n >= 2:
                    act.wait_ge(S("conv_silu"), n - 1)
                for q in range(2):
                    last = f(conv[n % 2][:, q, :], T(step)[:, q * SEQ:(q + 1) * SEQ], ACT.Identity,
                             scale=conv_w(3, ft + q), bias=conv_b(ft + q))
                last.then_inc(S("conv_first"), 1)

            def conv_silu(i, h):
                wait_read(act, ("xb", i, h))
                if i >= 3 and h == 0:
                    wait_full(act, ("xsn", i - 3, 1))
                dst = bcT[:, 4 * i + 2 * h:4 * i + 2 * h + 2, :] if i < 2 else xsT[:, 2 * h:2 * h + 2, :]
                f(dst, conv[h][:], ACT.Silu).then_inc(S("conv_silu"), 1)

            def steps(step):
                kind = step[0]
                if kind in ("xT", "memT"):
                    step_xT(step)
                elif kind == "dt":
                    dt_scan()
                elif kind == "cs":
                    wait_read(act, step)
                    f(dte, dte, ACT.Exp).then_inc(S("cs_exp"), 1)
                    f(ecs, cs[:, HEADS:2 * HEADS], ACT.Exp).then_inc(S("cs_exp"), 1)
                elif kind == "hT":
                    _, name, h = step
                    if name[:2] == "qm":
                        l = int(name[2])
                        dst, gain = qmT(l, 2 * h), vcol[:, MQ + l:MQ + l + 1]
                    elif name[:2] == "km":
                        l = int(name[2])
                        dst, gain = kmT[l][:, 2 * h:2 * h + 2, :], vcol[:, MK + l:MK + l + 1]
                    else:
                        base = 4 * int(name[1]) + 2 * h
                        dst = (qT if name[0] == "q" else kT)[:, base:base + 2, :]
                        gain = gq_scaled if name[0] == "q" else vcol[:, SK_:SK_ + 1]
                    wait_full(act, step)
                    read(step, f(dst.rearrange("p h t -> p (h t)"), T(step)[:], scale=gain))
                elif kind == "xb":
                    conv_first(step[1], step[2])
                elif kind == "silu":
                    conv_silu(step[1], step[2])
                elif kind == "xsn":
                    _, j, t = step
                    wait_full(act, step)
                    read(step, f(y[:, t, j * COLS:(j + 1) * COLS], T(step)[:]))
                elif kind == "Bn":
                    wait_full(act, step)
                    read(step, f(bn[:].rearrange("p g n -> p (g n)"), T(step)[:]))
                elif kind == "segm":
                    i = 2 * step[1] + step[2]
                    act.wait_ge(S("seg_diff"), i + 1)
                    s = segs[i % 3].rearrange("p h l -> p (h l)")
                    f(s, s, ACT.Exp).then_inc(S("seg_exp"), 1)
                elif kind == "st":
                    g = step[1]
                    wait_full(act, step)
                    if g:
                        wait_full(act, ("yo", g - 1))
                    read(step, f(state[:], T(step)[:, 0:GW]))
                elif kind == "gate":
                    half = step[1]
                    if half == 0:
                        wait_acc_read(act, BLOCK_ACC["z0"], 1)
                        for t in range(TOK):
                            f(zs[:, t, 0:COLS], zs[:, t, 0:COLS], ACT.Silu).then_inc(S("z_silu"), 1)
                    for g in (2 * half, 2 * half + 1):
                        act.wait_ge(S("gated"), g + 1)
                        for t in range(TOK):
                            at = 4 * half + 2 * t + g % 2
                            f(sq[:, 0:GW], y[:, t, g * GW:(g + 1) * GW], ACT.Square,
                              accum_out=ssqy[:, at:at + 1]).then_inc(S("y_ssq"), 1)
                            act.wait_ge(S("y_ssq"), TOK * g + t + 1)
                elif kind == "yT":
                    j = step[1]
                    wait_full(act, step)
                    for q in range(2):
                        last = f(oT_hi0[:, 2 * j + q, :], T(step)[:, q * SEQ:(q + 1) * SEQ],
                                 scale=vcol[:, NORM_G + 2 * j + q:NORM_G + 2 * j + q + 1])
                    last.then_inc(S("yT_hi"), 1)
                elif kind == "sc":
                    _, l, hp, t = step
                    i = SC_ORDER.index((l, hp, t))
                    act.wait_ge(S("score_max"), i + 1)
                    for h in range(2):
                        k = 4 * t + 2 * hp + h
                        last = f(pm[l][2 * hp + t][:, h, :], T(step)[:, h * MEM:(h + 1) * MEM], ACT.Exp,
                                 scale=SCALE, bias=mx[:, 2 * (i % 2) + h:2 * (i % 2) + h + 1], accum_out=sums[:, k:k + 1])
                        if h == 0:
                            link(last)
                    read(step, last)
                elif kind == "pT":
                    _, l, h = step
                    wait_full(act, step)
                    if h >= 2:
                        wait_full(act, ("mo", l, 0))
                    read(step, f(pmT[l][:, h % 2].rearrange("p m t -> p (m t)"), T(step)[:]))
                elif kind == "mo":
                    _, l, hp = step
                    wait_full(act, step)
                    f(oT_hi[l][:, 12 + 2 * hp:14 + 2 * hp, :].rearrange("p h t -> p (h t)"),
                      T(step)[:]).then_inc(S("mo_hi"), 1)
                elif kind == "ffnT":
                    _, l, j = step
                    wait_full(act, step)
                    f(uT_hi[:, 2 * j:2 * j + 2, :].rearrange("p k t -> p (k t)"), T(step)[:]).then_inc(S("uT_hi"), 1)
                elif kind == "z":
                    if step[1] == 0:
                        act.preload_act_table_set("natural_log_exp_and_others")
                    if step[1] % 2 == 0:
                        return
                    pair = (step[1] - 1, step[1])
                    for h in pair:
                        wait_full(act, ("z", h))
                        last = f(abuf[:, h % 2], T(("z", h))[:, 0:384], ACT.Abs)
                    link(last)
                    for h in pair:
                        last = f(abuf[:, h % 2], abuf[:, h % 2], ACT.Exp, scale=-1.0)
                    link(last)
                    for h in pair:
                        f(abuf[:, h % 2], abuf[:, h % 2], ACT.Ln, bias=1.0).then_inc(S("log1p"), 1)
                elif kind == "C":
                    b = lsb[:, step[1] % 4]
                    wait_read(act, step)
                    f(b, b, ACT.Exp).then_inc(S("w_exp"), 1)
                elif kind == "O":
                    wait_full(act, step)
                    f(oT_hi1[:, step[1], :], T(step)[:, 0:SEQ]).then_inc(S("O_hi"), 1)

            for u in range(-1, UNITS):
                if ("xT", 0, 0, 0) in PLAN[u] or u in ENDS and ENDS[u][0] == "rows":
                    if u == UNITS - 1:
                        break
                    for t in range(TOK):
                        if u >= 0:
                            split_to(u + 2 + t)
                        for step in PLAN[u]:
                            if step[0] == "xT" and step[2] == t:
                                steps(step)
                        if u < 0:
                            split_to(u + 3 + t)
                    split_to(u + 4)
                    if u == -1:
                        for t in range(TOK):
                            for h in range(2):
                                act.wait_ge(S(f"x_landed{t}{h}"), 16)
                        sum_squares(0, xr)
                    else:
                        i = ENDS[u][2]
                        act.wait_ge(S("x_added"), 4 * (i + 1))
                        sum_squares(i + 1, xr)
                    if u in (U_FFN0 - 1, U_FFN1 - 1):
                        act.preload_act_table_set("silu_and_others")
                    continue
                for step in PLAN[u]:
                    if step[0] in EARLY:
                        steps(step)
                split_to(u + 3)
                for step in PLAN[u]:
                    if step[0] in MIDDLE:
                        steps(step)
                if u in ENDS:
                    kind, a = ENDS[u][:2]
                    if kind == "block":
                        end_block(u, a, *ENDS[u][2:])
                    elif kind == "ffn":
                        l, j = ENDS[u][2:]
                        if j == 0:
                            act.wait_ge(S("rstd"), 3 + 2 * l)
                        for t in range(TOK):
                            wait_acc(act, u, t)
                            f(sg[:, j % 2, t, :], acc[a % 2][t][:, 0:256], ACT.Silu,
                              scale=rstd_x[2 * l + 1][:, t:t + 1]).then_inc(S("gate_silu"), 1)
                for step in PLAN[u]:
                    if step[0] not in EARLY + MIDDLE:
                        steps(step)
                if u == 3:
                    act.wait_ge(S("mem_landed"), 32)
                    sum_squares(4, memn)
            for t in range(TOK):
                for h in range(2):
                    act.wait_ge(S("x_added"), 13 + 2 * t + h)
                    c = slice(h * COLS, (h + 1) * COLS)
                    act.dma_start(out[0, t * P:(t + 1) * P, c], xr[:, t, c]).then_inc(S("out_written"), 16)
            act.wait_ge(S("out_written"), 64)

        @block.vector
        def _(dve):
            made = [0]

            def link(ins):
                made[0] += 1
                ins.then_inc(S("dve_seq"), 1)
                dve.wait_ge(S("dve_seq"), made[0])

            v = nc.vector
            split_at = [0]

            def split_to(u):
                while split_at[0] < min(u, UNITS):
                    w = split_at[0]
                    n = SRC[w][1]
                    dve.wait_ge(hi_ready, w + 1)
                    v.tensor_tensor(lo[w % RING][:, 0:n], raw[w % RING][:, 0:n],
                                    hi[w % RING][:, 0:n].bitcast(F), ALU.subtract).then_inc(lo_ready, 1)
                    split_at[0] += 1

            def rsqrt(dst, ssq, n, count, done, nth):
                a, h, t = v8[:, 0:n], h8[:, 0:n], t8[:, 0:n]
                link(v.tensor_scalar(a, ssq, 1.0 / count, EPS, ALU.mult, ALU.add))
                link(v.tensor_scalar(t.bitcast(I32), a.bitcast(I32), 1, None, ALU.logical_shift_right))
                link(v.tensor_scalar(h, a, -0.5, None, ALU.mult))
                link(v.tensor_scalar(dst.bitcast(I32), t.bitcast(I32), -1.0, float(0x5f3759df), ALU.mult, ALU.add))
                for i in range(3):
                    link(v.tensor_tensor(t, dst, dst, ALU.mult))
                    link(v.tensor_tensor(t, t, h, ALU.mult))
                    last = v.scalar_tensor_tensor(dst, t, 1.5, dst, ALU.add, ALU.mult)
                    if i < 2:
                        link(last)
                last.then_inc(done, 1)
                dve.wait_ge(done, nth)

            def row_norm(p, i):
                dve.wait_ge(S("x_ssq"), TOK * i)
                rsqrt(rstd_x[p], ssq_x, 2, D, S("rstd"), i)

            def input_tile(first):
                halves = [first[:-1] + (h,) for h in range(2)]
                mem_, t = first[0] == "memT", first[-2]
                for h, step in enumerate(halves):
                    g0 = XT_GAIN[4 if mem_ else step[1]] + 4 * h
                    wait_full(dve, step)
                    v.tensor_tensor(hg[h], T(step)[:].rearrange("p (k t) -> p k t", k=4),
                                    each(vcol[:, g0:g0 + 4], P), ALU.mult).then_inc(S("hg"), 1)
                for h, step in enumerate(halves):
                    sl = (slice(None), slice(4 * h, 4 * h + 4), slice(t * P, (t + 1) * P))
                    dve.wait_ge(S("aT_hi"), xt_index(step) + 1)
                    read(step, v.tensor_tensor((mT_lo if mem_ else aT_lo)[sl], hg[h],
                                               (mT_hi if mem_ else aT_hi)[sl].bitcast(F), ALU.subtract))

            def steps(step):
                kind = step[0]
                if kind == "par" and step[1] == 0:
                    wait_full(dve, step)
                    read(step, v.tensor_copy(vcol[:, MIX_G:MIX_G + 16], T(step)[:, 0:16]))
                    wait_read(dve, step)
                elif kind == "par":
                    wait_full(dve, step)
                    link(v.tensor_copy(vcol[:, 0:ROWS_A], T(step)[:, 0:ROWS_A]))
                    read(step, v.tensor_copy(vcol[:, ROWS_A:ROWS_A + ROWS_B], T(step)[:, P:P + ROWS_B]))
                    wait_read(dve, step)
                    link(v.tensor_scalar(gq_scaled, vcol[:, SQ_:SQ_ + 1], SCALE, None, ALU.mult))
                elif kind == "memT" and step[2] == 0:
                    input_tile(step)
                elif kind == "dt":
                    dve.wait_ge(S("head_vectors_landed"), 48)
                    for t in range(TOK):
                        wait_acc_read(dve, BLOCK_ACC["dtq0"], t)
                    b2 = dtv.rearrange("p (t h) -> p t h", t=TOK)
                    v.tensor_tensor(b2, b2, whole(bias_b, TOK), ALU.add).then_inc(S("dt_biased"), 1)
                    dve.wait_ge(S("dt_log"), 2)
                    link(v.scalar_tensor_tensor(dt, dtv, 0.0, dta, ALU.max, ALU.add))
                    v.scalar_tensor_tensor(da.rearrange("p (t h) -> p t h", t=TOK),
                                           dt.rearrange("p (t h) -> p t h", t=TOK), -1.0,
                                           whole(alog_b, TOK), ALU.mult, ALU.mult).then_inc(S("da"), 1)
                elif kind == "cs":
                    wait_full(dve, step)
                    link(v.tensor_copy(cs, T(step)[:, 0:2 * HEADS]))
                    read(step, v.tensor_tensor(dte, T(step)[:, 2 * HEADS:3 * HEADS], cs[:, 0:HEADS], ALU.subtract))
                    dve.wait_ge(S("cs_exp"), 2)
                    v.tensor_tensor(dte, dte, dt[:, 0:HEADS], ALU.mult).then_inc(S("dtdte"), 1)
                elif kind == "xb":
                    _, i, h = step
                    n = 2 * i + h
                    ft = CONV_TILES[i] + 2 * h
                    dve.wait_ge(S("conv_first"), n + 1)
                    for tap in (1, 2, 3):
                        for q in range(2):
                            c_ = conv[n % 2][:, q, tap:SEQ]
                            last = v.scalar_tensor_tensor(c_, T(step)[:, q * SEQ:(q + 1) * SEQ - tap],
                                                          conv_w(3 - tap, ft + q), c_, ALU.mult, ALU.add)
                            if tap == 3 and q == 1:
                                read(step, last)
                            elif q == 1:
                                link(last)
                elif kind == "G":
                    wait_full(dve, step)
                    a = step[1]
                    read(step, v.tensor_tensor(gm[:, 2 * a:2 * a + 2].rearrange("p g c l -> p (g c) l"),
                                               T(step)[:].rearrange("p (k l) -> p k l", k=4),
                                               whole(tle[:], 4), ALU.mult))
                elif kind == "csT":
                    wait_full(dve, step)
                    read(step, v.tensor_copy(vrow[0:TOK * HEADS, 2, :], T(step)[0:TOK * HEADS, 0:P]))
                elif kind == "seg":
                    _, g, c = step
                    i = 2 * g + c
                    dve.wait_ge(S(f"decays_landed{i % 3}"), 16 * (i // 3 + 1))
                    for h in range(HPG):
                        last = v.tensor_scalar(segs[i % 3][:, h, :], segs[i % 3][:, h, :],
                                               cs[:, heads_of(c, g, 1, h)], 0.0, ALU.subtract, ALU.min)
                    last.then_inc(S("seg_diff"), 1)
                elif kind == "segm":
                    _, g, c = step
                    i = 2 * g + c
                    dve.wait_ge(S("seg_exp"), i + 1)
                    s = segs[i % 3]
                    v.tensor_tensor(s, s, whole(gm[:, g, c, :], HPG), ALU.mult).then_inc(S("w_scan"), 1)
                elif kind == "yd":
                    _, g, c = step
                    yg = y[:, c, g * GW:(g + 1) * GW]
                    wait_full(dve, step)
                    dve.wait_ge(S("skip"), 2 * g + c + 1)
                    read(step, v.tensor_tensor(yg, T(step)[:, 0:GW], yg, ALU.add))
                elif kind == "yo":
                    g = step[1]
                    wait_full(dve, step)
                    if g:
                        dve.wait_ge(S("y_whole"), g)
                    read(step, v.tensor_tensor(yoff[:].rearrange("p (h n) -> p h n", n=HP),
                                               T(step)[:, 0:GW].rearrange("p (h n) -> p h n", n=HP),
                                               each(ecs[:, heads_of(0, g)], HP), ALU.mult))
                elif kind == "hT":
                    pass
                elif kind == "gate":
                    half = step[1]
                    if half == 0:
                        dve.wait_ge(S("z_silu"), TOK)
                    wait_acc_read(dve, BLOCK_ACC[("z1", "z2")[half]], 1)
                    dve.wait_ge(S("y_whole"), 2 * half + 2)
                    for g in (2 * half, 2 * half + 1):
                        s = slice(g * GW, (g + 1) * GW)
                        v.tensor_tensor(y[:, :, s], y[:, :, s], zs[:, :, s], ALU.mult).then_inc(S("gated"), 1)
                    dve.wait_ge(S("y_ssq"), TOK * 2 * (half + 1))
                    ryh = ry[:, 4 * half:4 * half + 4]
                    rsqrt(ryh, ssqy[:, 4 * half:4 * half + 4], 4, GW, S("y_rstd"), half + 1)
                    for t in range(TOK):
                        yt = y[:, t, 2 * half * GW:2 * (half + 1) * GW].rearrange("p (g n) -> p g n", n=GW)
                        v.tensor_tensor(yt, yt, each(ryh[:, 2 * t:2 * t + 2], GW), ALU.mult).then_inc(S("y_normed"), 1)
                elif kind == "yT":
                    j = step[1]
                    dve.wait_ge(S("yT_hi"), j + 1)
                    for q in range(2):
                        g = NORM_G + 2 * j + q
                        last = v.scalar_tensor_tensor(oT_lo0[:, 2 * j + q, :], T(step)[:, q * SEQ:(q + 1) * SEQ],
                                                      vcol[:, g:g + 1], oT_hi0[:, 2 * j + q, :].bitcast(F),
                                                      ALU.mult, ALU.subtract)
                    read(step, last)
                elif kind == "sc":
                    _, l, hp, t = step
                    i = SC_ORDER.index((l, hp, t))
                    wait_full(dve, step)
                    link(v.reduce_max(rsum[:, 0:2], T(step)[:].rearrange("p (h m) -> p h m", h=2), axis=AX.X))
                    if i >= 2:
                        wait_read(dve, ("sc",) + SC_ORDER[i - 2])
                    v.tensor_scalar(mx[:, 2 * (i % 2):2 * (i % 2) + 2], rsum, -SCALE, None,
                                    ALU.mult).then_inc(S("score_max"), 1)
                    dve.wait_ge(S("score_max"), i + 1)
                elif kind == "pn":
                    _, l, hp, t = step
                    i = SC_ORDER.index((l, hp, t))
                    wait_read(dve, ("sc",) + step[1:])
                    k = 4 * t + 2 * hp
                    link(v.reciprocal(rsum, sums[:, k:k + 2]))
                    pv = pm[l][2 * hp + t]
                    v.tensor_tensor(pv, pv, each(rsum, MEM), ALU.mult).then_inc(S("p_normed"), 1)
                    dve.wait_ge(S("p_normed"), i + 1)
                elif kind == "mo":
                    _, l, hp = step
                    dve.wait_ge(S("mo_hi"), 2 * l + hp + 1)
                    s = slice(12 + 2 * hp, 14 + 2 * hp)
                    read(step, v.tensor_tensor(oT_lo[l][:, s, :].rearrange("p h t -> p (h t)"), T(step)[:],
                                               oT_hi[l][:, s, :].bitcast(F).rearrange("p h t -> p (h t)"),
                                               ALU.subtract))
                elif kind == "ffnT":
                    _, l, j = step
                    dve.wait_ge(S("uT_hi"), FFN_BLOCKS * l + j + 1)
                    s = slice(2 * j, 2 * j + 2)
                    read(step, v.tensor_tensor(uT_lo[:, s, :].rearrange("p k t -> p (k t)"), T(step)[:],
                                               uT_hi[:, s, :].bitcast(F).rearrange("p k t -> p (k t)"),
                                               ALU.subtract))
                elif kind == "z":
                    h = step[1]
                    l1, ps = abuf[:, h % 2], T(step)[:, 0:384]
                    dve.wait_ge(S("log1p"), h + 1)
                    if h >= 2:
                        wait_full(dve, ("C", h - 2))
                    if h >= 4:
                        wait_full(dve, ("O", h - 4))
                    link(v.scalar_tensor_tensor(lsb[:, h % 4], ps, 0.0, l1, ALU.min, ALU.subtract))
                    read(step, v.scalar_tensor_tensor(spb[:, h % 2], ps, 0.0, l1, ALU.max, ALU.add))
                elif kind == "C":
                    h = step[1]
                    wait_full(dve, step)
                    read(step, v.tensor_tensor(lsb[:, h % 4], lsb[:, h % 4], T(step)[:, 0:384], ALU.subtract))
                elif kind == "O":
                    h = step[1]
                    dve.wait_ge(S("O_hi"), h + 1)
                    read(step, v.tensor_tensor(oT_lo1[:, h, :], T(step)[:, 0:SEQ],
                                               oT_hi1[:, h, :].bitcast(F), ALU.subtract))

            def head_norm(name):
                i = HEAD_NORMS.index(name)
                dve.wait_ge(S("squares"), i + 1)
                link(v.reduce_sum(ssq8, sq[:].rearrange("p (h n) -> p h n", n=P), axis=AX.X))
                rsqrt(r8, ssq8, 8, P, S("head_rstd"), i + 1)
                b = natb(name)[:].rearrange("p t (h n) -> p (t h) n", n=P)
                v.tensor_tensor(b, b, each(r8, P), ALU.mult).then_inc(S("nat_normed"), 1)

            for u in range(-1, UNITS):
                rows = u in ENDS and ENDS[u][0] == "rows"
                if u == -1 or rows:
                    if u == -1:
                        steps(("par", 0))
                    i = ENDS[u][2] + 1 if rows else 0
                    if rows:
                        split_to(u + 2)
                    for t in range(TOK):
                        for h in range(2 if rows else 0):
                            wait_acc(dve, u, 2 * t + h)
                            xs_ = xr[:, t, h * COLS:(h + 1) * COLS]
                            v.tensor_tensor(xs_, acc[(ENDS[u][1] + t) % 2][h][:], xs_,
                                            ALU.add).then_inc(S("x_added"), 1)
                        if rows:
                            split_to(u + 2 + t)
                        if u < UNITS - 1:
                            input_tile(("xT", i, t, 0))
                        if not rows:
                            split_to(u + 3 + t)
                    if u < UNITS - 1:
                        split_to(u + 4)
                        row_norm(i, i + 2 if i else 1)
                    continue
                for step in PLAN[u]:
                    if step[0] in EARLY:
                        steps(step)
                split_to(u + 3)
                for step in PLAN[u]:
                    if step[0] in MIDDLE:
                        steps(step)
                if u in ENDS:
                    kind, a = ENDS[u][:2]
                    name = ENDS[u][2]
                    if kind == "block" and (name in HEAD_NORMS or name == "dtq1"):
                        head_norm("qm0" if name == "dtq1" else name)
                    elif kind == "ffn":
                        l, j = ENDS[u][2:]
                        n = FFN_BLOCKS * l + j
                        if j >= 2:
                            wait_full(dve, ("ffnT", l, j - 2))
                        for t in range(TOK):
                            dve.wait_ge(S("gate_silu"), TOK * n + t + 1)
                            v.scalar_tensor_tensor(un[:, j % 2, t, :], acc[a % 2][t][:, 256:512],
                                                   rstd_x[2 * l + 1][:, t:t + 1], sg[:, j % 2, t, :],
                                                   ALU.mult, ALU.mult).then_inc(acc_free[a % 2], 1)
                for step in PLAN[u]:
                    if step[0] not in EARLY + MIDDLE:
                        steps(step)
                if u == 3:
                    row_norm(4, 2)

        @block.tensor
        def _(pe):
            mm = nc.tensor.matmul

            def begin(step):
                i = USES[step]
                if i >= 4:
                    pe.wait_ge(bank_read[i % 4], i // 4)
                return bank[i % 4]

            def tr(dst, src):
                return nc.tensor.transpose(dst, src, ident[:])

            def products(ps, stat_hi, stat_lo, mov_hi, mov_lo, first, last):
                mm(ps, stat_hi, mov_lo, start=first, stop=False)
                mm(ps, stat_hi, mov_hi, start=False, stop=False)
                return mm(ps, stat_lo, mov_hi, start=False, stop=last)

            def wait_acc_free(a, j):
                b = a - 2
                if b < 0:
                    return
                if b in MODE:
                    _, i, t = MODE[b]
                    pe.wait_ge(S("x_added"), 4 * i + 2 * t + j + 1)
                else:
                    wait_acc_read(pe, b, j)

            def col_products(u, a, half, t, width, act_hi, act_lo):
                s = u % RING
                pe.wait_ge(lo_ready, u + 1)
                if half == 0:
                    wait_acc_free(a, t)
                for k in range(UNIT_KT):
                    kt = half * UNIT_KT + k
                    tt, w = slice(t * P, (t + 1) * P), slice(k * width, (k + 1) * width)
                    last = products(acc[a % 2][t][:, 0:width], act_hi[:, kt, tt], act_lo[:, kt, tt],
                                    hi[s][:, w], lo[s][:, w], kt == 0, kt == KT - 1)
                return last

            def row_products(u, a, kt0, t, first, final, act_hi, act_lo):
                s = u % RING
                pe.wait_ge(lo_ready, u + 1)
                for h in range(2):
                    if first:
                        wait_acc_free(a + t, h)
                    for k in range(2):
                        tt, w = slice(t * P, (t + 1) * P), slice(k * D + h * COLS, k * D + (h + 1) * COLS)
                        last = products(acc[(a + t) % 2][h][:], act_hi[:, kt0 + k, tt], act_lo[:, kt0 + k, tt],
                                        hi[s][:, w], lo[s][:, w], first and k == 0, final and k == 1)
                    if final and (t, h) != (1, 1):
                        last.then_inc(acc_done, 1)
                return last

            def steps(step):
                kind = step[0]
                if kind in NO_BANK:
                    return
                b = begin(step)
                if kind == "par" and step[1] == 0:
                    pe.wait_ge(S("gain_landed"), 16)
                    pe.wait_ge(S("masks"), 4)
                    last = nc.tensor.transpose(b[:, 0:16], vrow[0:16, 2, :], ident[0:16, 0:16])
                elif kind == "par":
                    pe.wait_ge(S("vectors_landed"), 144)
                    pe.wait_ge(S("masks"), 4)
                    nc.tensor.transpose(b[:, 0:ROWS_A], vrow[0:ROWS_A, 0, :], ident[0:ROWS_A, 0:ROWS_A])
                    last = nc.tensor.transpose(b[:, P:P + ROWS_B], vrow[0:ROWS_B, 1, :], ident[0:ROWS_B, 0:ROWS_B])
                elif kind == "xT":
                    _, p, t, h = step
                    if p == 0:
                        pe.wait_ge(S(f"x_landed{t}{h}"), 16)
                    else:
                        pe.wait_ge(S("x_added"), 4 * (p - 1) + 2 * t + h + 1)
                    for k in range(4):
                        last = tr(b[:, k * P:(k + 1) * P], xr[:, t, (4 * h + k) * P:(4 * h + k + 1) * P])
                elif kind == "memT":
                    _, t, h = step
                    pe.wait_ge(S("mem_landed"), 32)
                    for k in range(4):
                        last = tr(b[:, k * P:(k + 1) * P], memn[:, t, (4 * h + k) * P:(4 * h + k + 1) * P])
                elif kind == "cs":
                    pe.wait_ge(S("da"), 1)
                    mm(b[:, 0:2 * HEADS], tle[:], da, start=True, stop=True)
                    last = mm(b[:, 2 * HEADS:3 * HEADS], ones[:], da[:, 0:HEADS], start=True, stop=True)
                elif kind == "csT":
                    wait_read(pe, ("cs",))
                    last = nc.tensor.transpose(b[0:TOK * HEADS, 0:P], cs, ident[:])
                elif kind == "hT":
                    _, name, h = step
                    pe.wait_ge(S("nat_normed"), HEAD_NORMS.index(name) + 1)
                    for q in range(2):
                        for t in range(TOK):
                            c0 = (2 * h + q) * P
                            last = tr(b[:, q * SEQ + t * P:q * SEQ + (t + 1) * P], natb(name)[:, t, c0:c0 + P])
                elif kind == "xb":
                    _, i, h = step
                    name = ["B", "C", "xs0", "xs1", "xs2"][i]
                    wait_acc_read_all(BLOCK_ACC[name])
                    for q in range(2):
                        for t in range(TOK):
                            c0 = (2 * h + q) * P
                            last = tr(b[:, q * SEQ + t * P:q * SEQ + (t + 1) * P], natb(name)[:, t, c0:c0 + P])
                elif kind == "Bn":
                    pe.wait_ge(S("conv_silu"), 2)
                    for g in range(GROUPS):
                        last = tr(b[:, g * P:(g + 1) * P], bcT[:, g, 0:P])
                elif kind == "xsn":
                    _, j, t = step
                    pe.wait_ge(S("conv_silu"), 2 * (j + 2) + 2)
                    for q in range(4):
                        last = tr(b[:, q * P:(q + 1) * P], xsT[:, q, t * P:(t + 1) * P])
                elif kind == "G":
                    pe.wait_ge(S("conv_silu"), 4)
                    for q in range(2):
                        g = 2 * step[1] + q
                        for c in range(2):
                            o = (2 * q + c) * P
                            last = mm(b[:, o:o + P], bcT[:, g, c * P:(c + 1) * P], bcT[:, 4 + g, c * P:(c + 1) * P],
                                      start=True, stop=True)
                elif kind == "yd":
                    _, g, c = step
                    i = 2 * g + c
                    pe.wait_ge(S("w_scan"), i + 1)
                    pe.wait_ge(S("xpad"), i + 1)
                    for j in range(HPG // 2):
                        for e in range(2):
                            last = mm(b[:, j * P:(j + 1) * P], segs[i % 3][:, 2 * j + e, :], xpad[:, c, 2 * j + e, :],
                                      start=(e == 0), stop=(e == 1))
                elif kind == "st":
                    g = step[1]
                    pe.wait_ge(S("xdte"), g + 1)
                    wait_read(pe, ("Bn",))
                    last = mm(b[:, 0:GW], bn[:, g, :], xdte[:], start=True, stop=True)
                elif kind == "yo":
                    g = step[1]
                    wait_read(pe, ("st", g))
                    last = mm(b[:, 0:GW], bcT[:, 4 + g, P:SEQ], state[:], start=True, stop=True)
                elif kind == "yT":
                    j = step[1]
                    pe.wait_ge(S("y_normed"), TOK * (j // 3 + 1))
                    for q in range(2):
                        for t in range(TOK):
                            c0 = (2 * j + q) * P
                            last = tr(b[:, q * SEQ + t * P:q * SEQ + (t + 1) * P], y[:, t, c0:c0 + P])
                elif kind == "sc":
                    _, l, hp, t = step
                    for h in range(2):
                        wait_read(pe, ("hT", f"km{l}", h))
                        wait_read(pe, ("hT", f"qm{l}", h))
                    for h in range(2):
                        hh = 2 * hp + h
                        last = mm(b[:, h * MEM:(h + 1) * MEM], qmT(l, 2 * hp)[:, h, t * P:(t + 1) * P], kmT[l][:, hh, :],
                                  start=True, stop=True)
                elif kind == "pT":
                    _, l, h = step
                    pe.wait_ge(S("p_normed"), 4 * l + 2 * (h // 2) + 2)
                    for m in range(2):
                        for t in range(TOK):
                            last = tr(b[:, m * SEQ + t * P:m * SEQ + (t + 1) * P],
                                      pm[l][2 * (h // 2) + t][:, h % 2, m * P:(m + 1) * P])
                elif kind == "mo":
                    _, l, hp = step
                    wait_acc_read_all(BLOCK_ACC[f"vm{l}"])
                    for h in range(2):
                        wait_read(pe, ("pT", l, 2 * hp + h))
                    for h in range(2):
                        c0 = (2 * hp + h) * P
                        for m in range(2):
                            last = mm(b[:, h * SEQ:(h + 1) * SEQ], vm[l][:, m, c0:c0 + P], pmT[l][:, h, m, :],
                                      start=(m == 0), stop=(m == 1))
                elif kind == "ffnT":
                    _, l, j = step
                    wait_acc_read_all((A_FFN0, A_FFN1)[l] + j)
                    for q in range(2):
                        for t in range(TOK):
                            last = tr(b[:, q * SEQ + t * P:q * SEQ + (t + 1) * P], un[:, j % 2, t, q * P:(q + 1) * P])
                elif kind == "z":
                    h = step[1]
                    for n in ("k", "q"):
                        wait_read(pe, ("hT", f"{n}{h // 4}", h % 4 // 2))
                    mm(b[:, 0:SEQ], kT[:, h, 0:P], qT[:, h, :], start=True, stop=True)
                    last = mm(b[:, SEQ:SEQ + P], kT[:, h, P:SEQ], qT[:, h, P:SEQ], start=True, stop=True)
                elif kind == "C":
                    h = step[1]
                    sp_ = spb[:, h % 2]
                    pe.wait_ge(S("sp_masked"), h + 1)
                    mm(b[:, 0:SEQ], tgt[:], sp_[:, 0:SEQ], start=True, stop=False)
                    mm(b[:, P:SEQ], ones[:], sp_[:, SEQ:SEQ + P], start=False, stop=True)
                    last = mm(b[:, SEQ:SEQ + P], tgt[:], sp_[:, SEQ:SEQ + P], start=True, stop=True)
                elif kind == "O":
                    h = step[1]
                    w = lsb[:, h % 4]
                    pe.wait_ge(S("w_masked"), h + 1)
                    if h % 4 == 0:
                        wait_acc_read_all(BLOCK_ACC[f"v{h // 4}"])
                    mm(b[:, 0:SEQ], vn[:, 0, h * P:(h + 1) * P], w[:, 0:SEQ], start=True, stop=False)
                    last = mm(b[:, P:SEQ], vn[:, 1, h * P:(h + 1) * P], w[:, SEQ:SEQ + P], start=False, stop=True)
                filled(step, last)

            def wait_acc_read_all(a):
                for t in range(TOK):
                    wait_acc_read(pe, a, t)

            def inputs_ready(p, t):
                for h in range(2):
                    wait_read(pe, ("memT", t, h) if p == 4 else ("xT", p, t, h))

            def column_phase(u0, a0, p, widths, memory=()):
                for i, width in enumerate(widths):
                    u, a = u0 + 2 * i, a0 + i
                    operand = (mT_hi, mT_lo) if i in memory else (aT_hi, aT_lo)
                    if i == 0:
                        inputs_ready(p, 0)
                        col_products(u, a, 0, 0, width, *operand)
                        for h in range(2):
                            steps(("xT", p, 1, h))
                        col_products(u + 1, a, 1, 0, width, *operand).then_inc(acc_done, 1)
                        inputs_ready(p, 1)
                        col_products(u, a, 0, 1, width, *operand).then_inc(unit_used, 1)
                        for step in PLAN[u]:
                            steps(step)
                        col_products(u + 1, a, 1, 1, width, *operand).then_inc(unit_used, 1)
                        for step in PLAN[u + 1]:
                            steps(step)
                        continue
                    if memory and i == min(memory):
                        for t in range(TOK):
                            inputs_ready(4, t)
                    for half in range(2):
                        last = col_products(u + half, a, half, 0, width, *operand)
                        if half == 1:
                            last.then_inc(acc_done, 1)
                        col_products(u + half, a, half, 1, width, *operand).then_inc(unit_used, 1)
                        for step in PLAN[u + half]:
                            steps(step)

            def row_phase(u0, a0, p, rows, needs, act_hi, act_lo):
                def part(i, t):
                    return row_products(u0 + i, a0, rows[i], t, i == 0, i == len(rows) - 1, act_hi, act_lo)

                n = len(rows)
                for i in range(n - 2):
                    for step in needs(rows[i]):
                        wait_read(pe, step)
                    part(i, 0)
                    part(i, 1).then_inc(unit_used, 1)
                    for step in PLAN[u0 + i]:
                        steps(step)
                for i in (n - 2, n - 1):
                    for step in needs(rows[i]):
                        wait_read(pe, step)
                    part(i, 0)
                part(n - 2, 1).then_inc(unit_used, 1)
                for h in range(2 if p else 0):
                    steps(("xT", p, 0, h))
                part(n - 1, 1).then_inc(unit_used, 1)

            def keep_warm(n):
                for _ in range(n):
                    mm(bank[3][:, 0:P], ones[:], ones[:], start=True, stop=True)

            pe.wait_ge(S("ones_made"), 1)
            keep_warm(7)
            for step in PLAN[-1]:
                if step[:1] + step[2:3] != ("xT", 1):
                    steps(step)
            keep_warm(10)
            column_phase(U_IN0, A_IN0, 0, [b[2] for b in IN0], [i for i, b in enumerate(IN0) if b[0][1:2] == "m"])
            row_phase(U_OUT0, A_OUT0, 1, OUT0_ROWS,
                      lambda kt: [("mo", 0, (kt - 12) // 2)] if kt >= 12 else [("yT", kt // 2)], oT_hi0, oT_lo0)
            column_phase(U_FFN0, A_FFN0, 1, [COLS] * FFN_BLOCKS)
            row_phase(U_DOWN0, A_DOWN0, 2, DOWN_ROWS, lambda kt: [("ffnT", 0, kt // 2)], uT_hi, uT_lo)
            column_phase(U_IN1, A_IN1, 2, [b[2] for b in IN1])
            row_phase(U_OUT1, A_OUT1, 3, OUT1_ROWS,
                      lambda kt: [("mo", 1, (kt - 12) // 2)] if kt >= 12 else [("O", kt), ("O", kt + 1)],
                      oT_hi1, oT_lo1)
            column_phase(U_FFN1, A_FFN1, 3, [COLS] * FFN_BLOCKS)
            row_phase(U_DOWN1, A_DOWN1, None, DOWN_ROWS, lambda kt: [("ffnT", 1, kt // 2)], uT_hi, uT_lo)


_INS = ["x", "mem", "mix_norm_g", "ffn_norm_g", "mem_norm_g", "mem_w_kv", "mem_q_norm_g", "mem_k_norm_g",
        "ssd_w_in", "ssd_conv_w", "ssd_conv_b", "ssd_dt_bias", "ssd_a_log", "ssd_d", "ssd_norm_g", "ssd_w_out",
        "sb_w_in", "sb_q_norm_g", "sb_k_norm_g", "sb_w_out", "ffn_w_gate_up", "ffn_w_down"]


def kernel(**inputs):
    import numpy as np
    import concourse.bacc as bacc
    from concourse.bass_utils import run_bass_kernel_spmd

    nc = bacc.Bacc("TRN2", target_bir_lowering=False, num_devices=1)
    arrays, args = {}, []
    for name in _INS:
        a = np.ascontiguousarray(inputs[name])
        arrays[f"in_{name}"] = a
        args.append(nc.dram_tensor(f"in_{name}", a.shape, mybir.dt.from_np(a.dtype), kind="ExternalInput").ap())
    out = nc.dram_tensor("out", (1, SEQ, D), mybir.dt.float32, kind="ExternalOutput").ap()
    trunk(nc, *args, out)
    return run_bass_kernel_spmd(nc, [arrays], core_ids=[0]).results[0]["out"]
```
